# Optimizing a Trainium2 kernel written in Bass

```python
import math
import jax
import jax.numpy as jnp
from jax import lax
import numpy as np

D_MODEL = 1024
BATCH = 1
SEQ = 512
DEPTH = 2
DEC_BATCH = 1
DEC_SEQ = 64
PAST_LEN = 1024

CHUNK = 64
N_MIXERS = 2
N_A = (DEPTH + 1) // 2
N_B = DEPTH // 2
SGU_CHUNK = 128
D_SGU = 2 * D_MODEL
SGU_GROUP_DIM = 128
SGU_GROUPS = D_SGU // SGU_GROUP_DIM
N_HEADS = 16
Q_LORA = 384
KV_LORA = 256
NOPE_DIM = 64
ROPE_DIM = 32
V_DIM = 64
QK_DIM = NOPE_DIM + ROPE_DIM
ATTN_SCALE = 1.0 / math.sqrt(QK_DIM)
ROPE_BASE = 10000.0
Q_BLOCK = 128
D_FF = 4 * D_MODEL
EPS = 1e-6
NEG_INF = -1e30

kernel_name = 'streaming_sgu_mla_hybrid_step'

def rms_norm(x, g):
    xf = x.astype(jnp.float32)
    y = xf * lax.rsqrt(jnp.mean(xf * xf, axis=-1, keepdims=True) + EPS)
    return (y * g.astype(jnp.float32)).astype(x.dtype)

def rope(x, pos):
    half = ROPE_DIM // 2
    inv = ROPE_BASE ** (-jnp.arange(half, dtype=jnp.float32) / half)
    ang = pos.astype(jnp.float32)[:, None] * inv[None, :]
    ang = ang.reshape((ang.shape[0],) + (1,) * (x.ndim - 3) + (half,))
    cos, sin = jnp.cos(ang), jnp.sin(ang)
    xf = x.astype(jnp.float32)
    x1, x2 = xf[..., :half], xf[..., half:]
    return jnp.concatenate([x1 * cos - x2 * sin, x1 * sin + x2 * cos], axis=-1).astype(x.dtype)

def chunk_causal_mask(n):
    c = jnp.arange(n) // CHUNK
    return c[:, None] >= c[None, :]

def sgu_mixer(h, w_in, norm_g, w_s, b_s, w_out, rows):
    B, S, _ = h.shape
    z = jax.nn.gelu(h @ w_in, approximate=False)
    u, v = jnp.split(z, 2, axis=-1)
    v = rms_norm(v, norm_g)
    ws = w_s[:, :rows, :rows] * chunk_causal_mask(rows).astype(w_s.dtype)[None]
    vg = v.reshape(B, S // rows, rows, SGU_GROUPS, SGU_GROUP_DIM)
    mixed = jnp.einsum('gij,bcjgd->bcigd', ws, vg) + b_s[:, :rows].T[None, None, :, :, None]
    y = u * mixed.reshape(B, S, D_SGU)
    return y @ w_out, v

def mla_project(h, pos, w_in, q_norm_g, kv_norm_g, w_uq, q_nope_g, q_rope_g, k_rope_g):
    B, S, _ = h.shape
    a = h @ w_in
    c_q, c_kv, k_r = jnp.split(a, [Q_LORA, Q_LORA + KV_LORA], axis=-1)
    c_q = rms_norm(c_q, q_norm_g)
    c_kv = rms_norm(c_kv, kv_norm_g)
    k_r = rope(rms_norm(k_r, k_rope_g), pos)
    q = (c_q @ w_uq).reshape(B, S, N_HEADS, QK_DIM)
    q_nope = rms_norm(q[..., :NOPE_DIM], q_nope_g)
    q_rope = rope(rms_norm(q[..., NOPE_DIM:], q_rope_g), pos)
    return q_nope, q_rope, c_kv, k_r

def mla_expand(c_kv, w_ukv, k_nope_g):
    B, S, _ = c_kv.shape
    kv = (c_kv @ w_ukv).reshape(B, S, N_HEADS, NOPE_DIM + V_DIM)
    k_nope = rms_norm(kv[..., :NOPE_DIM], k_nope_g)
    return k_nope, kv[..., NOPE_DIM:]

def mla_attend(q_nope, q_rope, k_nope, k_rope, v, mask):
    s = (jnp.einsum('bqhd,bkhd->bhqk', q_nope, k_nope, preferred_element_type=jnp.float32)
         + jnp.einsum('bqhr,bkr->bhqk', q_rope, k_rope, preferred_element_type=jnp.float32)) * ATTN_SCALE
    if mask is not None:
        s = jnp.where(mask, s, NEG_INF)
    p = jax.nn.softmax(s, axis=-1).astype(v.dtype)
    return jnp.einsum('bhqk,bkhd->bqhd', p, v)

def mla_prompt_attention(q_nope, q_rope, k_nope, k_rope, v):
    B, S = q_nope.shape[:2]
    nq = S // Q_BLOCK
    qn_b = q_nope.reshape(B, nq, Q_BLOCK, N_HEADS, NOPE_DIM).transpose(1, 0, 2, 3, 4)
    qr_b = q_rope.reshape(B, nq, Q_BLOCK, N_HEADS, ROPE_DIM).transpose(1, 0, 2, 3, 4)
    k_chunk = jnp.arange(S) // CHUNK

    def one_block(args):
        bi, qn, qr = args
        q_chunk = (bi * Q_BLOCK + jnp.arange(Q_BLOCK)) // CHUNK
        mask = k_chunk[None, :] <= q_chunk[:, None]
        return mla_attend(qn, qr, k_nope, k_rope, v, mask[None, None])

    o = lax.map(one_block, (jnp.arange(nq), qn_b, qr_b))
    return o.transpose(1, 0, 2, 3, 4).reshape(B, S, N_HEADS * V_DIM)

def sqrelu_mlp(h, w_up, w_down):
    return jnp.square(jax.nn.relu(h @ w_up)) @ w_down

def setup_inputs(seed: int = 0) -> dict:
    key = jax.random.key(seed)
    ks = jax.random.split(key, 24)

    def nrm(k, shape, scale):
        return jax.random.normal(k, shape, jnp.float32) * scale

    def gain(k, shape):
        return 1.0 + 0.1 * jax.random.normal(k, shape, jnp.float32)

    return {
        'x_prompt': nrm(ks[0], (BATCH, SEQ, D_MODEL), 1.0),
        'x_sample': nrm(ks[1], (DEC_BATCH, DEC_SEQ, D_MODEL), 1.0),
        'cache_kv_latent': nrm(ks[2], (N_B, DEC_BATCH, PAST_LEN, KV_LORA), 1.0),
        'cache_k_rope': nrm(ks[3], (N_B, DEC_BATCH, PAST_LEN, ROPE_DIM), 1.0),
        'mix_norm_g': gain(ks[4], (DEPTH, D_MODEL)),
        'mlp_norm_g': gain(ks[5], (DEPTH, D_MODEL)),
        'sgu_w_in': nrm(ks[6], (N_A, D_MODEL, 2 * D_SGU), D_MODEL ** -0.5),
        'sgu_norm_g': gain(ks[7], (N_A, D_SGU)),
        'sgu_w_s': nrm(ks[8], (N_A, SGU_GROUPS, SGU_CHUNK, SGU_CHUNK), 0.5 * SGU_CHUNK ** -0.5),
        'sgu_b_s': gain(ks[9], (N_A, SGU_GROUPS, SGU_CHUNK)),
        'sgu_w_out': nrm(ks[10], (N_A, D_SGU, D_MODEL), D_SGU ** -0.5),
        'mla_w_in': nrm(ks[11], (N_B, D_MODEL, Q_LORA + KV_LORA + ROPE_DIM), D_MODEL ** -0.5),
        'mla_q_norm_g': gain(ks[12], (N_B, Q_LORA)),
        'mla_kv_norm_g': gain(ks[13], (N_B, KV_LORA)),
        'mla_w_uq': nrm(ks[14], (N_B, Q_LORA, N_HEADS * QK_DIM), Q_LORA ** -0.5),
        'mla_w_ukv': nrm(ks[15], (N_B, KV_LORA, N_HEADS * (NOPE_DIM + V_DIM)), KV_LORA ** -0.5),
        'mla_q_nope_g': gain(ks[16], (N_B, NOPE_DIM)),
        'mla_q_rope_g': gain(ks[17], (N_B, ROPE_DIM)),
        'mla_k_nope_g': gain(ks[18], (N_B, NOPE_DIM)),
        'mla_k_rope_g': gain(ks[19], (N_B, ROPE_DIM)),
        'mla_w_o': nrm(ks[20], (N_B, N_HEADS * V_DIM, D_MODEL), (N_HEADS * V_DIM) ** -0.5),
        'mlp_w_up': nrm(ks[21], (DEPTH, D_MODEL, D_FF), D_MODEL ** -0.5),
        'mlp_w_down': nrm(ks[22], (DEPTH, D_FF, D_MODEL), D_FF ** -0.5),
    }

def reference(x_prompt, x_sample, cache_kv_latent, cache_k_rope, mix_norm_g, mlp_norm_g,
              sgu_w_in, sgu_norm_g, sgu_w_s, sgu_b_s, sgu_w_out,
              mla_w_in, mla_q_norm_g, mla_kv_norm_g, mla_w_uq, mla_w_ukv,
              mla_q_nope_g, mla_q_rope_g, mla_k_nope_g, mla_k_rope_g, mla_w_o,
              mlp_w_up, mlp_w_down):
    n_prompt = x_prompt.shape[1]
    n_new = x_sample.shape[1]
    pos_prompt = jnp.arange(n_prompt)
    pos_sample = PAST_LEN + jnp.arange(n_new)
    xp, xs = x_prompt, x_sample
    lat_p, kr_p, lat_s, kr_s, sgu_v_s = [], [], [], [], []
    for i in range(DEPTH):
        j = i // N_MIXERS
        hp = rms_norm(xp, mix_norm_g[i])
        hs = rms_norm(xs, mix_norm_g[i])
        if i % N_MIXERS == 0:
            sgu_w = (sgu_w_in[j], sgu_norm_g[j], sgu_w_s[j], sgu_b_s[j], sgu_w_out[j])
            mp, _ = sgu_mixer(hp, *sgu_w, SGU_CHUNK)
            ms, v_new = sgu_mixer(hs, *sgu_w, n_new)
            sgu_v_s.append(v_new)
        else:
            proj = (mla_w_in[j], mla_q_norm_g[j], mla_kv_norm_g[j], mla_w_uq[j],
                    mla_q_nope_g[j], mla_q_rope_g[j], mla_k_rope_g[j])
            qn, qr, c, kr = mla_project(hp, pos_prompt, *proj)
            kn, v = mla_expand(c, mla_w_ukv[j], mla_k_nope_g[j])
            mp = mla_prompt_attention(qn, qr, kn, kr, v) @ mla_w_o[j]
            lat_p.append(c)
            kr_p.append(kr)
            qn, qr, c, kr = mla_project(hs, pos_sample, *proj)
            c_all = jnp.concatenate([cache_kv_latent[j], c], axis=1)
            kr_all = jnp.concatenate([cache_k_rope[j], kr], axis=1)
            kn, v = mla_expand(c_all, mla_w_ukv[j], mla_k_nope_g[j])
            o = mla_attend(qn, qr, kn, kr_all, v, None)
            ms = o.reshape(o.shape[0], n_new, N_HEADS * V_DIM) @ mla_w_o[j]
            lat_s.append(c)
            kr_s.append(kr)
        xp = xp + mp
        xs = xs + ms
        xp = xp + sqrelu_mlp(rms_norm(xp, mlp_norm_g[i]), mlp_w_up[i], mlp_w_down[i])
        xs = xs + sqrelu_mlp(rms_norm(xs, mlp_norm_g[i]), mlp_w_up[i], mlp_w_down[i])
    new_kv_latent_prompt = jnp.stack(lat_p)
    new_k_rope_prompt = jnp.stack(kr_p)
    new_kv_latent_sample = jnp.stack(lat_s)
    new_k_rope_sample = jnp.stack(kr_s)
    new_sgu_v_sample = jnp.stack(sgu_v_s)
    return (xp, xs, new_kv_latent_prompt, new_k_rope_prompt, new_kv_latent_sample, new_k_rope_sample, new_sgu_v_sample)


_drawn_inputs = setup_inputs


def setup_inputs(seed=0):
    import zlib

    import numpy as np

    out = dict(_drawn_inputs(seed))
    spreads = {}
    factors = {'cache_k_rope': 3.539,
     'mla_q_norm_g': 8.0,
     'mla_q_nope_g': 8.0,
     'mla_q_rope_g': 8.0,
     'mla_k_nope_g': 8.0}
    for name, (base, spread) in spreads.items():
        noise = np.random.default_rng([zlib.crc32(name.encode()), seed]).standard_normal(out[name].shape)
        drawn = base * np.exp(spread * noise) if base else spread * noise
        out[name] = jnp.asarray(drawn.astype(out[name].dtype))
    for name, factor in factors.items():
        out[name] = (out[name] * factor).astype(out[name].dtype)
    return out
```

```python
from contextlib import ExitStack

import numpy as np

import concourse.bass as bass
from concourse import mybir

F32 = mybir.dt.float32
F32R = mybir.dt.float32r
ALU = mybir.AluOpType
ACT = mybir.ActivationFunctionType
AX_X = mybir.AxisListType.X

P = 128
D = 1024
KD = D // P
SEQ, DEC, PAST = 512, 64, 1024
T = SEQ + DEC
TH = T // 2
NT = 5
ROWS = [P] * 4 + [DEC]
CHUNK = 64
DS = 2 * D
GROUPS = DS // P
DFF = 4 * D
HEADS, NOPE, ROPE, VD = 16, 64, 32, 64
QK = NOPE + ROPE
QL, KL = 384, 256
KEYS = SEQ + PAST + DEC
KT_N = 13
SKEYS = PAST + DEC
EPS = 1e-6
MASKED = -1e30
SCALE = 1.0 / float(QK) ** 0.5

HG = 4
NG = HEADS // HG
UNIT = 1024
SLOTS = 4
SCRATCH = 25088

U_V = 0
U_SGU = 16
U_MLP0 = 48
U_IN = 112
U_GRP = 120
U_O = 136
U_MLP1 = 144
UNITS = 208
F_SGU, F_MLP0, F_O, F_MLP1 = 0, 32, 96, 104
B_SGU, B_MLP0, B_O, B_MLP1 = 0, 16, 48, 56

ITEMS = []
for _pair in range(2):
    for _h in (2 * _pair, 2 * _pair + 1):
        ITEMS += [("prompt", _h, b) for b in range(4)]
    ITEMS.append(("sample", _pair, 0))
NI = len(ITEMS)
SAMPLE_AT = [i for i, it in enumerate(ITEMS) if it[0] == "sample"]
PIECES = []
for _i, (_kind, _a, _b) in enumerate(ITEMS):
    if _kind == "prompt":
        PIECES.append((_i, list(range(_b + 1))))
    else:
        PIECES += [(_i, [0, 1, 2, 3]), (_i, [4, 5, 6, 7]), (_i, [8])]
NP = len(PIECES)
PIECES_OF = [[p for p, (i, _) in enumerate(PIECES) if i == it] for it in range(NI)]
EVEN_PIECES = (NP + 1) // 2
OUTS = [("prompt", 0), ("prompt", 1), ("sample", 0), ("prompt", 2), ("prompt", 3), ("sample", 1)]
NO = len(OUTS)


def out_of(item):
    kind, a, _ = ITEMS[item]
    return OUTS.index((kind, a))


def attention_order():
    steps = [("score", 0), ("score", 1), ("key", 11), ("key", 12)]
    owed, turned = None, 0

    def item_pieces(i):
        nonlocal owed
        for p in PIECES_OF[i]:
            steps.append(("turn", p))
            if owed is not None:
                steps.append(("pv", owed))
            owed = p

    for i in range(2, NI):
        steps.append(("score", i))
        item_pieces(i - 2)
        if i == SAMPLE_AT[0] + 5:
            steps.append(("gather", 0))
    item_pieces(NI - 2)
    item_pieces(NI - 1)
    steps.append(("pv", owed))
    steps.append(("gather", 1))
    return steps


ORDER = attention_order()


def build_trunk(nc, xt, gains, stream, ws, bs, sgu_gcol, sgu_grow, cache_ct, cache_krt, lat_g, q_nope_g,
                q_rope_g, k_nope_g, rope_cs, mask_rows, out_x, out_kv, out_kr, out_v):
    with ExitStack() as ctx:
        sem_of = lambda name: ctx.enter_context(nc.semaphore(name))

        cursor = [0]

        def region(size):
            at = cursor[0]
            cursor[0] += (size + 31) // 32 * 32
            return at

        base0 = nc.sbuf_base
        cursor[0] = (base0 + 31) // 32 * 32

        def place(name, shape, dt, at):
            return nc.alloc_sbuf_tensor_at(name, shape, dt, offset=at)

        def new(name, shape, dt=F32):
            return place(name, shape, dt, region(4 * int(np.prod(shape[1:]))))

        x = new("x", [P, KD, T])
        a_at = region(2 * 4 * KD * T)
        h_hi = place("h_hi", [P, KD, T], F32R, a_at)
        h_lo = place("h_lo", [P, KD, T], F32R, a_at + 4 * KD * T)
        kT = place("kT", [P, HG, KEYS], F32, a_at)
        qT = place("qT", [P, HG, T], F32, a_at + 4 * HG * KEYS)
        b_at = region(2 * 4 * KD * T)
        hid_hi = place("hid_hi", [P, KD, T], F32R, b_at)
        hid_lo = place("hid_lo", [P, KD, T], F32R, b_at + 4 * KD * T)
        lat = place("lat", [P, NT, QL + KL + ROPE], F32, b_at)
        LAT = QL + KL + ROPE
        lat_g_bc = place("lat_g_bc", [P, LAT], F32, b_at + 4 * NT * LAT)
        krr = place("krr", [P, NT, QK], F32, b_at + 4 * (NT + 1) * LAT)
        raw = new("raw", [P, SLOTS, UNIT])
        w_hi = new("w_hi", [P, SLOTS, UNIT], F32R)
        w_lo = new("w_lo", [P, SLOTS, UNIT], F32R)
        v_at = region(4 * NT * DS)
        v = place("v", [P, NT, DS], F32, v_at)
        cT_hi = place("cT_hi", [P, 2, KEYS], F32R, v_at)
        cT_lo = place("cT_lo", [P, 2, KEYS], F32R, v_at + 8 * KEYS)
        cqT_hi = place("cqT_hi", [P, 3, T], F32R, v_at + 16 * KEYS)
        cqT_lo = place("cqT_lo", [P, 3, T], F32R, v_at + 16 * KEYS + 12 * T)
        s_at = region(4 * KT_N * HG * VD)
        ws_sb = place("ws_sb", [P, 8, P], F32, s_at)
        b_bc = place("b_bc", [P, 8, P], F32, s_at + 4096)
        vn = place("vn", [P, 2, NT, P], F32, s_at + 8192)
        cache_raw = place("cache_raw", [P, 2, PAST], F32, s_at)
        vals = place("vals", [P, KT_N, HG * VD], F32, s_at)
        r_at = region(SCRATCH)
        bump = [r_at]

        def scratch(name, shape, dt=F32):
            at = bump[0]
            bump[0] += (4 * int(np.prod(shape[1:])) + 31) // 32 * 32
            assert bump[0] <= r_at + SCRATCH, name
            return place(name, shape, dt, at)

        rms_bc = scratch("rms_bc", [P, T])
        sq_sum = scratch("sq_sum", [P, T])
        act_t = scratch("act_t", [P, 2, T])
        mixed = scratch("mixed", [P, T])
        diag = scratch("diag", [P, NT, P])
        v_out = scratch("v_out", [DEC, DS])
        junk = scratch("junk", [P, 512])
        bump[0] = r_at
        q_tok = scratch("q_tok", [P, NT, HG, QK])
        rope_a = scratch("rope_a", [P, NT, HG, ROPE])
        rope_b = scratch("rope_b", [P, NT, HG, ROPE])
        end_projection = bump[0]
        bump[0] = r_at
        probs = scratch("probs", [P, 2, SEQ])
        probs_s = scratch("probs_s", [P, SKEYS])
        turned = scratch("turned", [P, 2, SEQ])
        bump[0] = max(bump[0], end_projection)
        k_norm = scratch("k_norm", [P, 2, HG, NOPE])
        k_sq = scratch("k_sq", [P, 2, HG * NOPE])
        q_sq = scratch("q_sq", [P, 2, HG * QK])
        o_tok = scratch("o_tok", [P, 2, NT, P])
        ident = new("ident", [P, P])
        ones = new("ones", [P, P])
        gains_sb = new("gains_sb", [P, 4, KD])
        sgu_g = new("sgu_g", [P, GROUPS])
        gq_row = new("gq_row", [P, ROPE])
        gq_col = new("gq_col", [P, 1])
        gk_col = new("gk_col", [P, 1])
        cs_q = new("cs_q", [P, 2, NT, ROPE])
        cs_sb = new("cs_sb", [P, 2, NT, ROPE])
        var_tok = new("var_tok", [P, NT])
        inv_tok = new("inv_tok", [P, NT])
        rms_tok = new("rms_tok", [P, NT])
        ss_v = new("ss_v", [P, NT, 4])
        ss_v1 = new("ss_v1", [P, NT])
        rms_v = new("rms_v", [P, NT])
        ss_lat = new("ss_lat", [P, 3, NT])
        rms_lat = new("rms_lat", [P, 3, NT])
        ss_q = new("ss_q", [P, NT, HG, 3])
        ss_q2 = new("ss_q2", [P, NT, HG])
        rms_q = new("rms_q", [P, NT, HG, 3])
        ss_k = new("ss_k", [P, 2, HG])
        rms_k = new("rms_k", [P, 2, HG])
        neg_max = new("neg_max", [P, NI])
        sums = new("sums", [P, NI])
        inv_sums = new("inv_sums", [P, NI])
        assert cursor[0] <= nc.sbuf_usable_end, (cursor[0], nc.sbuf_usable_end)

        ps = ctx.enter_context(nc.psum_tensor("ps", [P, 8, 512], F32))

        x_loaded = [sem_of(f"x_loaded{k}") for k in range(KD)]
        const_loaded = sem_of("const_loaded")
        half_loaded = sem_of("half_loaded")
        cache_loaded = sem_of("cache_loaded")
        rows_loaded = sem_of("rows_loaded")
        stored = sem_of("stored")
        raw_loaded = [sem_of(f"raw_loaded{i}") for i in range(SLOTS)]
        split_hi = sem_of("split_hi")
        split_lo = sem_of("split_lo")
        unit_done = sem_of("unit_done")
        ones_set = sem_of("ones_set")
        set_up = sem_of("set_up")
        ident_zero = sem_of("ident_zero")
        ident_set = sem_of("ident_set")
        tile_read = sem_of("tile_read")
        h_hi_set = sem_of("h_hi_set")
        h_ready = sem_of("h_ready")
        x_sq = sem_of("x_sq")
        sq_added = sem_of("sq_added")
        stat_summed = sem_of("stat_summed")
        var_set = sem_of("var_set")
        inv_set = sem_of("inv_set")
        rms_set = sem_of("rms_set")
        diag_set = sem_of("diag_set")
        rms_spread = sem_of("rms_spread")
        rms_bc_set = sem_of("rms_bc_set")
        tok_done = sem_of("tok_done")
        tok_read = sem_of("tok_read")
        v_set = sem_of("v_set")
        ss_v_set = sem_of("ss_v_set")
        rms_v_step = sem_of("rms_v_step")
        rms_v_set = sem_of("rms_v_set")
        v_out_set = sem_of("v_out_set")
        vn_ready = sem_of("vn_ready")
        u_set = sem_of("u_set")
        mix_done = sem_of("mix_done")
        mix_read = sem_of("mix_read")
        y_set = sem_of("y_set")
        hid_sq = sem_of("hid_sq")
        hid_hi_set = sem_of("hid_hi_set")
        hid_ready = sem_of("hid_ready")
        cache_hi = sem_of("cache_hi")
        cache_split = sem_of("cache_split")
        ss_lat_set = sem_of("ss_lat_set")
        lat_step = sem_of("lat_step")
        rms_lat_set = sem_of("rms_lat_set")
        lat_ready = sem_of("lat_ready")
        krr_step = sem_of("krr_step")
        lat_turned = sem_of("lat_turned")
        lat_hi = sem_of("lat_hi")
        lat_split = sem_of("lat_split")
        kr_turned = sem_of("kr_turned")
        kr_set = sem_of("kr_set")
        gq_step = sem_of("gq_step")
        q_done = sem_of("q_done")
        q_sq_set = sem_of("q_sq_set")
        q_read = sem_of("q_read")
        q_step = sem_of("q_step")
        q_step_d = sem_of("q_step_d")
        rms_q_set = sem_of("rms_q_set")
        q_roped = sem_of("q_roped")
        q_ready = sem_of("q_ready")
        q_turned = sem_of("q_turned")
        qT_set = sem_of("qT_set")
        kv_done = sem_of("kv_done")
        k_sq_set = sem_of("k_sq_set")
        vals_set = sem_of("vals_set")
        ss_k_set = sem_of("ss_k_set")
        k_step = sem_of("k_step")
        rms_k_set = sem_of("rms_k_set")
        k_ready = sem_of("k_ready")
        k_turned = sem_of("k_turned")
        kT_set = sem_of("kT_set")
        scored = sem_of("scored")
        max_set = sem_of("max_set")
        probs_set = sem_of("probs_set")
        piece_turned = sem_of("piece_turned")
        piece_even = sem_of("piece_even")
        piece_odd = sem_of("piece_odd")
        pv_done = sem_of("pv_done")
        inv_sums_set = sem_of("inv_sums_set")
        o_read = sem_of("o_read")
        o_gathered = sem_of("o_gathered")

        ds = bass.ds
        TILE_BANKS = (2, 0)
        STAT = 7
        SETUPS = 6
        CONSTS = 7

        def halves(a):
            return a.rearrange("p (n c) -> p n c", n=2)

        def tile_psum(slot):
            b = TILE_BANKS[slot]
            return ps[:, b:b + 2, 0:TH]

        def cols(t):
            return slice(t * P, t * P + ROWS[t])

        def bank_of(chunk, t):
            return t - 3 if t >= 3 else 2 + 3 * (chunk % 2) + t

        def key_rows(j):
            return P if j < KT_N - 1 else DEC

        def key_at(j):
            return j * P


        def latent_target(L):
            t = L % NT
            if L < NT:
                return cqT_hi, cqT_lo, t * P
            return cT_hi, cT_lo, (t * P if t < 4 else SEQ + PAST)

        def take_piece(eng, copy, p, g, piece_set):
            item, tiles = PIECES[p]
            sample_end = ITEMS[item][0] == "sample" and tiles == [8]
            r, w = (DEC, P) if sample_end else (P, len(tiles) * P)
            eng.wait_ge(piece_turned, g * NP + (p + 1))
            if p >= 2:
                eng.wait_ge(pv_done, g * NP + (p - 1))
            copy(turned[0:r, p % 2, 0:w], ps[0:r, 5 + p % 2, 0:w]).then_inc(piece_set, 1)

        def piece_set(p):
            return piece_odd if p % 2 else piece_even

        def pieces_by(p):
            return NP - EVEN_PIECES if p % 2 else EVEN_PIECES

        block = ctx.enter_context(nc.Block())

        @block.sync
        def _(sp):
            for u in range(SLOTS):
                sp.dma_start(raw[:, u, :], stream[u]).then_inc(raw_loaded[u], 16)
            with sp.Fori(1, UNITS // SLOTS, 1) as i:
                for u in range(SLOTS):
                    sp.wait_ge(split_lo, (i - 1) * SLOTS + u + 1)
                    sp.dma_start(raw[:, u, :], stream[i * SLOTS + u]).then_inc(raw_loaded[u], 16)

        @block.gpsimd
        def _(pool):
            loads, units = pool.alloc_register("loads"), pool.alloc_register("units")
            nc.gpsimd.memset(ident[:], 0.0).then_inc(ident_zero, 1)
            nc.gpsimd.memset(ones[:], 1.0).then_inc(ones_set, 1)
            nc.gpsimd.memset(var_tok[:], 1.0).then_inc(set_up, 1)
            nc.gpsimd.memset(ss_v[:], 1.0).then_inc(set_up, 1)
            nc.gpsimd.memset(ss_lat[:], 1.0).then_inc(set_up, 1)
            nc.gpsimd.memset(ss_q[:], 1.0).then_inc(set_up, 1)
            nc.gpsimd.memset(ss_k[:], 1.0).then_inc(set_up, 1)
            pool.wait_ge(ident_zero, 1)
            nc.gpsimd.affine_select(out=ident[:], in_=ident[:], compare_op=ALU.not_equal, fill=1.0, base=0,
                                    pattern=[[-1, P]], channel_multiplier=1).then_inc(ident_set, 1)

            def split(u, n, i, first=False):
                if not first:
                    pool.reg_mov(loads, i * 16 + 16)
                    pool.reg_mov(units, n - SLOTS + 1)
                    pool.wait_ge(ident_zero, 1)
                    pool.wait_ge(unit_done, units)
                pool.wait_ge(raw_loaded[u], 16 if first else loads)
                nc.gpsimd.tensor_scalar(w_hi[:, u, :], raw[:, u, :], 1.0, 0.0, ALU.mult, ALU.add).then_inc(split_hi, 1)
                pool.wait_ge(split_hi, n + 1)
                nc.gpsimd.tensor_tensor(w_lo[:, u, :], raw[:, u, :], w_hi[:, u, :].bitcast(F32),
                                        ALU.subtract).then_inc(split_lo, 1)

            for u in range(SLOTS):
                split(u, u, 0, first=True)
            with pool.Fori(1, (U_GRP + SLOTS) // SLOTS, 1) as i:
                for u in range(SLOTS):
                    split(u, i * SLOTS + u, i)

            def rope_products(tiles, rows):
                n = tiles.stop - tiles.start
                part = q_tok[0:rows, tiles, :, NOPE:QK]
                a, b = rope_a[0:rows, tiles], rope_b[0:rows, tiles]

                def table(which, lo, hi):
                    return cs_q[0:rows, which, tiles, lo:hi].unsqueeze(2).broadcast_to([rows, n, HG, hi - lo])

                h = ROPE // 2
                nc.gpsimd.tensor_tensor(a, part, table(0, 0, ROPE), ALU.mult).then_inc(q_step, 1)
                nc.gpsimd.tensor_tensor(b[:, :, :, 0:h], part[:, :, :, h:ROPE], table(1, 0, h),
                                        ALU.mult).then_inc(q_step, 1)
                nc.gpsimd.tensor_tensor(b[:, :, :, h:ROPE], part[:, :, :, 0:h], table(1, h, ROPE),
                                        ALU.mult).then_inc(q_step, 1)

            with pool.Fori(0, NG, 1) as g:
                pool.wait_ge(rms_q_set, g + 1)
                for t in range(NT):
                    r = ROWS[t]
                    q3 = q_tok[0:r, t].rearrange("p h (s c) -> p (h s) c", c=ROPE)
                    w3 = rms_q[0:r, t].rearrange("p h s -> p (h s)").unsqueeze(2).broadcast_to([r, 3 * HG, ROPE])
                    nc.gpsimd.tensor_tensor(q3, q3, w3, ALU.mult).then_inc(q_step, 1)
                pool.wait_ge(q_step, g * 11 + 5)
                rope_products(slice(0, 4), P)
                rope_products(slice(4, 5), DEC)
                pool.wait_ge(q_step, g * 11 + 11)
                for tiles, rows in ((slice(0, 4), P), (slice(4, 5), DEC)):
                    nc.gpsimd.tensor_tensor(q_tok[0:rows, tiles, :, NOPE:QK], rope_a[0:rows, tiles],
                                            rope_b[0:rows, tiles], ALU.add).then_inc(q_ready, 1)
                for u in range(SLOTS):
                    split(u, g * SLOTS + (U_GRP + SLOTS + u), g + (U_GRP + SLOTS) // SLOTS)
            with pool.Fori(U_O // SLOTS + 1, UNITS // SLOTS, 1) as i:
                for u in range(SLOTS):
                    split(u, i * SLOTS + u, i)

        @block.tensor
        def _(pe):
            filled, freed = pe.alloc_register("filled"), pe.alloc_register("freed")
            def three(out, l_hi, l_lo, r_hi, r_lo, first, last):
                nc.tensor.matmul(out, l_hi, r_hi, start=first, stop=False)
                nc.tensor.matmul(out, l_hi, r_lo, start=False, stop=False)
                return nc.tensor.matmul(out, l_lo, r_hi, start=False, stop=last)

            def feature_tile(u, f, n, operand, ready, count, middle=None):
                pe.wait_ge(split_lo, n + 1)
                pe.wait_ge(tile_read, f + 1)
                pe.wait_ge(ready, count - 1)
                o_hi, o_lo = operand
                for k in range(KD):
                    if k == KD - 1:
                        pe.wait_ge(ready, count)
                    if k == KD // 2 and middle:
                        middle()
                    for n2 in range(2):
                        tok = slice(n2 * TH, n2 * TH + TH)
                        last = three(tile_psum(u % 2)[:, n2, :], w_hi[:, u, k * P:(k + 1) * P],
                                     w_lo[:, u, k * P:(k + 1) * P], o_hi[:, k, tok], o_lo[:, k, tok],
                                     k == 0, k == KD - 1)
                last.then_inc(unit_done, 1)

            H = (h_hi, h_lo)
            HID = (hid_hi, hid_lo)

            def norm_sums(s):
                pe.wait_ge(sq_added, 9 * s + 9)
                for t in range(NT):
                    last = nc.tensor.matmul(ps[0:ROWS[t], STAT, t:t + 1], sq_sum[:, cols(t)], ones[:, 0:1],
                                            start=True, stop=True)
                last.then_inc(stat_summed, 1)

            def norm_spread(n):
                pe.wait_ge(diag_set, n + 1)
                for t in range(NT):
                    r = ROWS[t]
                    out = ps[:, 5, t * P:(t + 1) * P] if t < 4 else ps[:, 6, 0:DEC]
                    last = nc.tensor.matmul(out, ones[0:r, :], diag[0:r, t, 0:r], start=True, stop=True)
                last.then_inc(rms_spread, 1)

            def token_chunk(chunk, parity, first_unit, width, between=None):
                for j in range(4):
                    pe.wait_ge(split_lo, first_unit + j + 1)
                    for t in range(NT):
                        if j == 0:
                            pe.wait_ge(tok_read, chunk * 5 + t + (1 if t < 3 else 6))
                        for k2 in range(2):
                            k = 2 * j + k2
                            w = slice(k2 * 512, k2 * 512 + width)
                            last = three(ps[0:ROWS[t], bank_of(parity, t), 0:width], h_hi[:, k, cols(t)],
                                         h_lo[:, k, cols(t)], w_hi[:, j, w], w_lo[:, j, w], k == 0, k == KD - 1)
                        if j == 3 and t < NT - 1:
                            last.then_inc(tok_done, 1)
                    last.then_inc(unit_done, 1)
                    if j == 0 and between:
                        between()

            pe.sem_inc(tile_read, 2)
            pe.sem_inc(tok_read, 10)
            pe.sem_inc(mix_read, 4)

            pe.wait_ge(ones_set, 1)
            norm_sums(0)
            norm_spread(0)
            pe.wait_ge(h_ready, KD)
            pe.wait_ge(var_set, 2)
            with pe.Fori(0, 2, 1) as c2:
                token_chunk(c2 * 2, 0, c2 * 8, 512)
                pe.wait_ge(rms_bc_set, 2)
                token_chunk(c2 * 2 + 1, 1, c2 * 8 + 4, 512)
            with pe.Fori(0, 2, 1) as half:
                pe.reg_mov(filled, half * 48 + 48)
                pe.wait_ge(set_up, SETUPS)
                pe.wait_ge(half_loaded, filled)
                with pe.Fori(0, 2, 1) as i:
                    for u in range(4):
                        f = half * 16 + i * 4 + u
                        g = half * 8 + i * 4 + u
                        m = i * 4 + u
                        feature_tile(u, f, f + U_SGU, H, h_ready, KD)
                        pe.wait_ge(tok_read, 10 + 20)
                        pe.wait_ge(vn_ready, g * 2 + 2)
                        pe.wait_ge(mix_read, g * 2 + 2)
                        b = 4 + 2 * (u % 2)
                        for t in range(NT):
                            r = ROWS[t]
                            out = ps[:, b, t * P:(t + 1) * P] if t < 4 else ps[:, b + 1, 0:DEC]
                            last = nc.tensor.matmul(out, vn[0:r, u % 2, t, :],
                                                    ws_sb[0:r, ds(m, 1), 0:r].rearrange("p o i -> p (o i)"),
                                                    start=True, stop=True)
                        last.then_inc(mix_done, 1)
                with pe.Fori(0, 2, 1) as i:
                    for u in range(4):
                        f = half * 16 + i * 4 + (8 + u)
                        feature_tile(u, f, f + U_SGU, HID, hid_ready, half * 8 + (B_SGU + 8))

            def mlp(f0, n0, b0, h_count, s, spread_n):
                def sums():
                    norm_sums(s)

                for m in range(8):
                    feature_tile(m % 4, f0 + m, n0 + m, H, h_ready, h_count,
                                 middle=(lambda: norm_spread(spread_n)) if m == 1 else None)
                    if m == 0:
                        norm_sums(s)

                def down(q):
                    with pe.Fori(0, 2, 1) as i:
                        for u in range(4):
                            feature_tile(u, q * 16 + i * 4 + (f0 + 8 + u), q * 16 + i * 4 + (n0 + 8 + u),
                                         HID, hid_ready, q * 8 + (b0 + 8))

                down(0)
                with pe.Fori(1, 4, 1) as q:
                    with pe.Fori(0, 2, 1) as i:
                        for u in range(4):
                            feature_tile(u, q * 16 + i * 4 + (f0 + u), q * 16 + i * 4 + (n0 + u),
                                         H, h_ready, h_count)
                    down(q)

            mlp(F_MLP0, U_MLP0, B_MLP0, 2 * KD, 1, 1)

            pe.wait_ge(h_ready, 3 * KD - 1)
            pe.wait_ge(tile_read, F_O + 2)

            def after_first_unit():
                norm_sums(2)

            pe.wait_ge(h_ready, 3 * KD)
            token_chunk(4, 0, U_IN, QL, between=after_first_unit)
            pe.wait_ge(var_set, 6)
            token_chunk(5, 1, U_IN + 4, KL + ROPE)
            for L in range(2 * NT):
                t = L % NT
                r = ROWS[t]
                n_k, at = (3, 0) if L < NT else (2, QL)
                pe.wait_ge(lat_ready, L + 1)
                if L >= 3:
                    pe.wait_ge(lat_split, L - 2)
                for k in range(n_k):
                    last = nc.tensor.transpose(ps[:, 2 + L % 3, k * P:k * P + r],
                                               lat[0:r, t, at + k * P:at + (k + 1) * P], ident[0:r, 0:r])
                last.then_inc(lat_turned, 1)
            pe.wait_ge(krr_step, 9)
            for t in range(NT):
                r = ROWS[t]
                out = ps[0:QK, 0, t * P:(t + 1) * P] if t < 4 else ps[0:QK, 1, 0:DEC]
                last = nc.tensor.transpose(out, krr[0:r, t, :], ident[0:r, 0:r])
                if t >= 3:
                    last.then_inc(kr_turned, 1)

            pe.wait_ge(kr_set, 2)
            pe.wait_ge(lat_split, 2 * NT)
            pe.wait_ge(cache_split, 2)
            pe.wait_ge(rows_loaded, 48)
            with pe.Fori(0, NG, 1) as g:
                pe.wait_ge(hid_ready, g * 2 + B_O)
                for k in range(3):
                    pe.wait_ge(split_lo, g * 4 + (U_GRP + k + 1))
                    for t in range(NT):
                        last = three(ps[0:ROWS[t], t, 0:HG * QK], cqT_hi[:, k, cols(t)], cqT_lo[:, k, cols(t)],
                                     w_hi[:, k, 0:HG * QK], w_lo[:, k, 0:HG * QK], k == 0, k == 2)
                        if k == 2 and t < NT - 1:
                            last.then_inc(q_done, 1)
                    last.then_inc(unit_done, 1)
                pe.wait_ge(split_lo, g * 4 + (U_GRP + 4))

                def turn_keys(j):
                    r = key_rows(j)
                    pe.reg_mov(filled, g * KT_N + (j + 1))
                    pe.reg_mov(freed, g * KT_N + (j - 1) if j >= 2 else g * NT + NT)
                    pe.wait_ge(ident_set, 1)
                    pe.wait_ge(k_ready, filled)
                    pe.wait_ge(kT_set if j >= 2 else q_read, freed)
                    for h in range(HG):
                        last = nc.tensor.transpose(ps[0:NOPE, 2 + j % 2, h * P:h * P + r],
                                                   k_norm[0:r, j % 2, h, :], ident[0:r, 0:r])
                    last.then_inc(k_turned, 1)

                for j in range(KT_N):
                    r = key_rows(j)
                    keys = slice(key_at(j), key_at(j) + r)
                    if j >= 3:
                        pe.wait_ge(k_ready, g * KT_N + (j - 2))
                    for k in range(2):
                        w = slice(k * 512, (k + 1) * 512)
                        last = three(ps[0:r, 5 + j % 3, :], cT_hi[:, k, keys], cT_lo[:, k, keys],
                                     w_hi[:, 3, w], w_lo[:, 3, w], k == 0, k == 1)
                    last.then_inc(kv_done if j < KT_N - 1 else unit_done, 1)
                    if j >= 2:
                        turn_keys(j - 2)
                    if j >= 8:
                        t = j - 8
                        rq = ROWS[t]
                        pe.reg_mov(filled, g * 2 + 2)
                        if t >= 2:
                            pe.reg_mov(freed, g * NT + (t - 1))
                        pe.wait_ge(ident_set, 1)
                        pe.wait_ge(q_ready, filled)
                        if t >= 2:
                            pe.wait_ge(qT_set, freed)
                        for h in range(HG):
                            last = nc.tensor.transpose(ps[0:QK, t % 2, h * P:h * P + rq], q_tok[0:rq, t, h, :],
                                                       ident[0:rq, 0:rq])
                        last.then_inc(q_turned, 1)

                def score(i):
                    kind, a, blk = ITEMS[i]
                    if kind == "prompt":
                        n = 4 * a + blk
                        if n >= 2:
                            before = [x for x in range(i) if ITEMS[x][0] == "prompt"][-2]
                            pe.wait_ge(probs_set, g * NI + (before + 1))
                        rows = slice(blk * P, (blk + 1) * P)
                        if blk:
                            nc.tensor.matmul(ps[:, n % 2, 0:blk * P], qT[0:QK, a, rows], kT[0:QK, a, 0:blk * P],
                                             start=True, stop=True)
                        last = nc.tensor.matmul(ps[:, n % 2, rows], qT[0:QK + 1, a, rows], kT[0:QK + 1, a, rows],
                                                start=True, stop=True)
                    else:
                        if a:
                            pe.wait_ge(hid_ready, g * 2 + (B_O + 1))
                        for hh in range(2):
                            out = slice(hh * 64, hh * 64 + 64)
                            for n in range(3):
                                w = min(512, SKEYS - n * 512)
                                at = SEQ + n * 512
                                last = nc.tensor.matmul(ps[out, 2 + n, 0:w], qT[0:QK, 2 * a + hh, SEQ:T],
                                                        kT[0:QK, 2 * a + hh, at:at + w], start=True, stop=True)
                    last.then_inc(scored, 1)

                def turn(p):
                    item, tiles = PIECES[p]
                    kind, a, blk = ITEMS[item]
                    pe.reg_mov(filled, g * NI + (item + 1))
                    pe.reg_mov(freed, g * KT_N + KT_N if p < 2 else g * pieces_by(p) + p // 2)
                    pe.wait_ge(ident_set, 1)
                    pe.wait_ge(probs_set, filled)
                    pe.wait_ge(k_ready if p < 2 else piece_set(p), freed)
                    for n, kt in enumerate(tiles):
                        if kind == "prompt":
                            src, w = probs[:, (4 * a + blk) % 2, kt * P:(kt + 1) * P], P
                        else:
                            w = min(P, SKEYS - kt * P)
                            src = probs_s[:, kt * P:kt * P + w]
                        last = nc.tensor.transpose(ps[0:w, 5 + p % 2, n * P:(n + 1) * P], src, ident[:])
                    last.then_inc(piece_turned, 1)

                def times_values(p):
                    item, tiles = PIECES[p]
                    kind, a, blk = ITEMS[item]
                    o = out_of(item)
                    new_output = p == PIECES_OF[item][0] and o and out_of(PIECES[p - 1][0]) != o
                    pe.reg_mov(filled, g * pieces_by(p) + (p // 2 + 1))
                    if new_output:
                        pe.reg_mov(freed, g * NO + o)
                    elif p == 0:
                        pe.reg_mov(freed, g * KT_N + KT_N)
                    pe.wait_ge(ident_set, 1)
                    pe.wait_ge(piece_set(p), filled)
                    if new_output:
                        pe.wait_ge(o_read, freed)
                    elif p == 0:
                        pe.wait_ge(vals_set, freed)
                    for n, kt in enumerate(tiles):
                        if kind == "prompt":
                            last = nc.tensor.matmul(ps[:, 7, blk * VD:(blk + 1) * VD],
                                                    turned[:, p % 2, n * P:(n + 1) * P],
                                                    vals[:, kt, a * VD:(a + 1) * VD],
                                                    start=(kt == 0), stop=(kt == blk))
                        else:
                            w = min(P, SKEYS - kt * P)
                            for hh in range(2):
                                h = 2 * a + hh
                                last = nc.tensor.matmul(ps[hh * 64:hh * 64 + 64, 7, 0:VD],
                                                        turned[0:w, p % 2, n * P + hh * 64:n * P + hh * 64 + 64],
                                                        vals[0:w, 4 + kt, h * VD:(h + 1) * VD],
                                                        start=(kt == 0), stop=(kt == 8))
                    last.then_inc(pv_done, 1)

                def gather(pair):
                    pe.reg_mov(filled, g * NO + 3 * (pair + 1))
                    pe.wait_ge(ident_set, 1)
                    pe.wait_ge(o_read, filled)
                    for t in range(NT):
                        r = ROWS[t]
                        out = ps[:, 2, t * P:(t + 1) * P] if t < 4 else ps[:, 3, 0:DEC]
                        last = nc.tensor.transpose(out, o_tok[0:r, pair, t, :], ident[0:r, 0:r])
                        if t >= 3:
                            last.then_inc(o_gathered, 1)

                pe.wait_ge(qT_set, g * NT + NT)
                for step, n in ORDER:
                    if step == "score":
                        if n == 2:
                            pe.wait_ge(kT_set, g * KT_N + KT_N)
                        elif n < 2:
                            pe.wait_ge(kT_set, g * KT_N + 4)
                        score(n)
                    elif step == "key":
                        turn_keys(n)
                    elif step == "turn":
                        turn(n)
                    elif step == "pv":
                        times_values(n)
                    else:
                        gather(n)

            pe.wait_ge(hid_ready, B_O + 8)
            with pe.Fori(0, 2, 1) as i:
                for u in range(4):
                    feature_tile(u, i * 4 + (F_O + u), i * 4 + (U_O + u), HID, hid_ready, B_O + 8)

            mlp(F_MLP1, U_MLP1, B_MLP1, 4 * KD, 3, 2)

        @block.vector
        def _(dve):
            def norm_stats(s):
                dve.wait_ge(stat_summed, s + 1)
                nc.vector.tensor_scalar(var_tok[:, 0:4], ps[:, STAT, 0:4], 1.0 / D, EPS, ALU.mult,
                                        ALU.add).then_inc(var_set, 1)
                nc.vector.tensor_scalar(var_tok[0:DEC, 4:5], ps[0:DEC, STAT, 4:5], 1.0 / D, EPS, ALU.mult,
                                        ALU.add).then_inc(var_set, 1)
                dve.wait_ge(var_set, 2 * s + 2)
                nc.vector.reciprocal(inv_tok[:], var_tok[:]).then_inc(inv_set, 1)

            def norm_diagonal(s):
                dve.wait_ge(rms_set, s + 1)
                for t in range(NT):
                    r = ROWS[t]
                    last = nc.vector.tensor_scalar(diag[0:r, t, 0:r], ident[0:r, 0:r], rms_tok[0:r, t:t + 1], None,
                                                   ALU.mult)
                last.then_inc(diag_set, 1)

            def clear_sums():
                nc.vector.memset(sq_sum[:], 0.0).then_inc(sq_added, 1)

            def next_operand(m, slot, s):
                dve.wait_ge(h_hi_set, m + (8 * s + 1))
                xm, hm, lm = x[:, ds(m, 1), :], h_hi[:, ds(m, 1), :], h_lo[:, ds(m, 1), :]
                nc.vector.scalar_tensor_tensor(out=lm, in0=xm, scalar=gains_sb[:, s, ds(m, 1)],
                                               in1=hm.bitcast(F32), op0=ALU.mult,
                                               op1=ALU.subtract).then_inc(h_ready, 1)
                dve.wait_ge(x_sq, m + (8 * s + 1))
                dve.wait_ge(sq_added, m + (9 * s + 1))
                nc.vector.tensor_tensor(sq_sum[:], sq_sum[:], act_t[:, slot, :], ALU.add).then_inc(sq_added, 1)

            def add_to_x(u, m, f, n):
                dve.wait_ge(unit_done, n + 1)
                dve.wait_ge(tile_read, f + 2)
                xm = x[:, ds(m, 1), :].rearrange("p o (n c) -> p (o n) c", n=2)
                nc.vector.tensor_tensor(xm, tile_psum(u % 2), xm, ALU.add).then_inc(tile_read, 1)

            nc.vector.memset(ws_sb[CHUNK:P, :, 0:CHUNK], 0.0).then_inc(set_up, 1)
            dve.wait_ge(const_loaded, 16 * CONSTS)
            clear_sums()
            for k in range(KD):
                next_operand(k, k % 2, 0)
            dve.wait_ge(set_up, SETUPS)
            dve.wait_ge(ident_set, 1)
            norm_stats(0)
            norm_diagonal(0)

            dve.wait_ge(ss_v_set, 4 * NT)
            nc.vector.reduce_sum(ss_v1[:], ss_v[:], AX_X).then_inc(rms_v_step, 1)
            dve.wait_ge(rms_v_step, 1)
            nc.vector.tensor_scalar(ss_v1[:], ss_v1[:], 1.0 / DS, EPS, ALU.mult, ALU.add).then_inc(rms_v_step, 1)
            dve.wait_ge(rms_v_step, 2)
            nc.vector.reciprocal(ss_v1[:], ss_v1[:]).then_inc(rms_v_step, 1)
            dve.wait_ge(rms_v_set, 1)
            dve.wait_ge(rms_bc_set, 2)

            def gate(half):
                dve.wait_ge(half_loaded, half * 48 + 48)
                with dve.Fori(0, 2, 1) as i:
                    for u in range(4):
                        slot = u % 2
                        m = i * 4 + u
                        g = i * 4 + (half * 8 + u)
                        f = i * 4 + (half * 16 + u)
                        for tiles, r in ((slice(0, 4), P), (slice(4, 5), DEC)):
                            n = tiles.stop - tiles.start
                            nc.vector.tensor_tensor(vn[0:r, slot, tiles, :], v[0:r, tiles, ds(g * P, P)],
                                                    rms_v[0:r, tiles].unsqueeze(2).broadcast_to([r, n, P]),
                                                    ALU.mult).then_inc(vn_ready, 1)
                        dve.wait_ge(unit_done, f + (U_SGU + 1))
                        nc.vector.tensor_tensor(halves(act_t[:, slot, :]), tile_psum(slot), halves(rms_bc[:]),
                                                ALU.mult).then_inc(tile_read, 1)
                        dve.wait_ge(mix_done, g + 1)
                        b = 4 + 2 * slot
                        bias = b_bc[:, ds(m, 1), :]
                        nc.vector.scalar_tensor_tensor(
                            out=mixed[:, 0:SEQ].rearrange("p (c i) -> p c i", c=4),
                            in0=ps[:, b, :].rearrange("p (c i) -> p c i", c=4), scalar=sgu_g[:, ds(g, 1)],
                            in1=bias.broadcast_to([P, 4, P]), op0=ALU.mult, op1=ALU.add).then_inc(mix_read, 1)
                        nc.vector.scalar_tensor_tensor(
                            out=mixed[:, SEQ:T].unsqueeze(1), in0=ps[:, b + 1:b + 2, 0:DEC],
                            scalar=sgu_g[:, ds(g, 1)], in1=bias[:, :, 0:DEC], op0=ALU.mult,
                            op1=ALU.add).then_inc(mix_read, 1)
                        dve.wait_ge(u_set, g + 1)
                        dve.wait_ge(mix_read, g * 2 + 6)
                        nc.vector.tensor_tensor(mixed[:], mixed[:], act_t[:, slot, :], ALU.mult).then_inc(y_set, 1)
                        dve.wait_ge(hid_hi_set, g + 1)
                        nc.vector.tensor_tensor(hid_lo[:, ds(m, 1), :], mixed[:].unsqueeze(1),
                                                hid_hi[:, ds(m, 1), :].bitcast(F32),
                                                ALU.subtract).then_inc(hid_ready, 1)

            def project_back(f0, n0, last_s=None):
                if last_s is not None:
                    clear_sums()
                with dve.Fori(0, 2, 1) as i:
                    for u in range(4):
                        m = i * 4 + u
                        add_to_x(u, m, m + f0, m + n0)
                        if last_s is not None:
                            next_operand(m, u % 2, last_s)

            gate(0)
            nc.vector.scalar_tensor_tensor(out=v_out[:], in0=v[0:DEC, 4, :], scalar=rms_v[0:DEC, 4:5],
                                           in1=v_out[:], op0=ALU.mult, op1=ALU.mult).then_inc(v_out_set, 1)
            project_back(8, U_SGU + 8)
            gate(1)
            project_back(24, U_SGU + 24, last_s=1)

            def mlp(f0, n0, b0, s, spread_n, last_s):
                norm_stats(s)
                norm_diagonal(s)
                dve.wait_ge(rms_bc_set, 2 * spread_n + 2)

                def up(q):
                    with dve.Fori(0, 2, 1) as i:
                        for u in range(4):
                            m = i * 4 + u
                            dve.wait_ge(unit_done, q * 16 + m + (n0 + 1))
                            nc.vector.scalar_tensor_tensor(
                                out=halves(act_t[:, u % 2, :]), in0=tile_psum(u % 2), scalar=0.0,
                                in1=halves(rms_bc[:]), op0=ALU.max, op1=ALU.mult).then_inc(tile_read, 1)
                            dve.wait_ge(hid_hi_set, q * 8 + m + (b0 + 1))
                            nc.vector.tensor_tensor(hid_lo[:, ds(m, 1), :], act_t[:, u % 2, :].unsqueeze(1),
                                                    hid_hi[:, ds(m, 1), :].bitcast(F32),
                                                    ALU.subtract).then_inc(hid_ready, 1)

                with dve.Fori(0, 3, 1) as q:
                    up(q)
                    project_back(q * 16 + (f0 + 8), q * 16 + (n0 + 8))
                up(3)
                project_back(f0 + 56, n0 + 56, last_s=last_s)

            mlp(F_MLP0, U_MLP0, B_MLP0, 1, 1, 2)

            dve.wait_ge(stored, 16)
            half = ROPE // 2
            nc.vector.memset(krr[:, :, 0:NOPE], 0.0).then_inc(krr_step, 1)
            nc.vector.scalar_tensor_tensor(out=gq_col[0:NOPE, :], in0=gq_col[0:NOPE, :], scalar=SCALE,
                                           in1=gk_col[0:NOPE, :], op0=ALU.mult, op1=ALU.mult).then_inc(gq_step, 1)
            nc.vector.memset(gq_col[NOPE:QK, :], SCALE).then_inc(gq_step, 1)
            nc.vector.tensor_tensor(cs_q[:, 0], cs_sb[:, 0], gq_row[:].unsqueeze(1).broadcast_to([P, NT, ROPE]),
                                    ALU.mult).then_inc(gq_step, 1)
            for lo, other in ((0, half), (half, 0)):
                nc.vector.tensor_tensor(cs_q[:, 1, :, lo:lo + half], cs_sb[:, 1, :, lo:lo + half],
                                        gq_row[:, other:other + half].unsqueeze(1).broadcast_to([P, NT, half]),
                                        ALU.mult).then_inc(gq_step, 1)
            for k in range(2):
                dve.wait_ge(cache_hi, k + 1)
                nc.vector.tensor_tensor(cT_lo[:, k, SEQ:SEQ + PAST], cache_raw[:, k, :],
                                        cT_hi[:, k, SEQ:SEQ + PAST].bitcast(F32),
                                        ALU.subtract).then_inc(cache_split, 1)
            norm_stats(2)

            parts = [(0, QL), (QL, KL), (QL + KL, ROPE)]
            steps = 0
            for sums_wanted, which in ((5, (0,)), (15, (1, 2))):
                dve.wait_ge(ss_lat_set, sums_wanted)
                for w in which:
                    nc.vector.tensor_scalar(ss_lat[:, w, :], ss_lat[:, w, :], 1.0 / parts[w][1], EPS, ALU.mult,
                                            ALU.add).then_inc(lat_step, 1)
                steps += len(which)
                dve.wait_ge(lat_step, steps)
                lo, hi = which[0], which[-1] + 1
                nc.vector.reciprocal(ss_lat[:, lo:hi, :], ss_lat[:, lo:hi, :]).then_inc(lat_step, 1)
                steps += 1
                dve.wait_ge(rms_lat_set, 1 if which == (0,) else 2)
                for w in which:
                    at, width = parts[w]
                    for t in range(NT):
                        r = ROWS[t]
                        piece = lat[0:r, t, at:at + width]
                        nc.vector.scalar_tensor_tensor(out=piece, in0=piece, scalar=rms_lat[0:r, w, t:t + 1],
                                                       in1=lat_g_bc[0:r, at:at + width], op0=ALU.mult,
                                                       op1=ALU.mult).then_inc(lat_ready, 1)
            dve.wait_ge(lat_ready, 3 * NT)
            for tiles, r in ((slice(0, 4), P), (slice(4, 5), DEC)):
                k_in = lat[0:r, tiles, QL + KL:QL + KL + ROPE]
                a, b = rope_a[0:r, tiles, 0, :], rope_b[0:r, tiles, 0, :]
                nc.vector.tensor_tensor(a, k_in, cs_sb[0:r, 0, tiles, :], ALU.mult).then_inc(krr_step, 1)
                nc.vector.tensor_tensor(b[:, :, 0:half], k_in[:, :, half:ROPE], cs_sb[0:r, 1, tiles, 0:half],
                                        ALU.mult).then_inc(krr_step, 1)
                nc.vector.tensor_tensor(b[:, :, half:ROPE], k_in[:, :, 0:half], cs_sb[0:r, 1, tiles, half:ROPE],
                                        ALU.mult).then_inc(krr_step, 1)
            dve.wait_ge(krr_step, 7)
            for tiles, r in ((slice(0, 4), P), (slice(4, 5), DEC)):
                nc.vector.tensor_tensor(krr[0:r, tiles, NOPE:QK], rope_a[0:r, tiles, 0, :], rope_b[0:r, tiles, 0, :],
                                        ALU.add).then_inc(krr_step, 1)
            for L in range(2 * NT):
                t = L % NT
                r = ROWS[t]
                hi, lo, at = latent_target(L)
                n_k = 3 if L < NT else 2
                dve.wait_ge(lat_hi, L + 1)
                nc.vector.tensor_tensor(lo[:, :, at:at + r],
                                        ps[:, 2 + L % 3, 0:n_k * P].rearrange("p (k c) -> p k c", k=n_k)[:, :, 0:r],
                                        hi[:, :, at:at + r].bitcast(F32), ALU.subtract).then_inc(lat_split, 1)

            dve.wait_ge(gq_step, 5)
            with dve.Fori(0, NG, 1) as g:
                for t in range(NT):
                    r = ROWS[t]
                    dve.wait_ge(q_sq_set, g * NT + (t + 1))
                    nc.vector.reduce_sum(ss_q[0:r, t].rearrange("p h s -> p (h s)"),
                                         q_sq[0:r, t % 2, :].rearrange("p (s c) -> p s c", c=ROPE),
                                         AX_X).then_inc(q_step_d, 1)
                    nc.vector.tensor_copy(q_tok[0:r, t].rearrange("p h c -> p (h c)"),
                                          ps[0:r, t, 0:HG * QK]).then_inc(q_read, 1)
                dve.wait_ge(q_step_d, g * 9 + 5)
                nc.vector.tensor_tensor(ss_q2[:], ss_q[:, :, :, 0], ss_q[:, :, :, 1], ALU.add).then_inc(q_step_d, 1)
                dve.wait_ge(q_step_d, g * 9 + 6)
                nc.vector.tensor_scalar(ss_q[:, :, :, 0:2], ss_q2[:].unsqueeze(3).broadcast_to([P, NT, HG, 2]),
                                        1.0 / NOPE, EPS, ALU.mult, ALU.add).then_inc(q_step_d, 1)
                nc.vector.tensor_scalar(ss_q[:, :, :, 2], ss_q[:, :, :, 2], 1.0 / ROPE, EPS, ALU.mult,
                                        ALU.add).then_inc(q_step_d, 1)
                dve.wait_ge(q_step_d, g * 9 + 8)
                nc.vector.reciprocal(ss_q[:], ss_q[:]).then_inc(q_step_d, 1)

                def norm_keys(j):
                    r = key_rows(j)
                    dve.wait_ge(rms_k_set, g * KT_N + (j + 1))
                    if j >= 2:
                        dve.wait_ge(k_turned, g * KT_N + (j - 1))
                    nc.vector.tensor_tensor(
                        k_norm[0:r, j % 2], ps[0:r, 5 + j % 3, 0:HG * NOPE].rearrange("p (h c) -> p h c", h=HG),
                        rms_k[0:r, j % 2].unsqueeze(2).broadcast_to([r, HG, NOPE]), ALU.mult).then_inc(k_ready, 1)

                def take_queries(t):
                    r = ROWS[t]
                    dve.wait_ge(q_turned, g * NT + (t + 1))
                    nc.vector.tensor_scalar(
                        qT[0:QK, :, cols(t)], ps[0:QK, t % 2, :].rearrange("p (h c) -> p h c", h=HG)[:, :, 0:r],
                        gq_col[0:QK, 0:1], None, ALU.mult).then_inc(qT_set, 1)

                for j in range(KT_N):
                    r = key_rows(j)
                    base = g * (3 * KT_N) + 3 * j
                    dve.wait_ge(k_sq_set, g * KT_N + (j + 1))
                    nc.vector.reduce_sum(ss_k[0:r, j % 2], k_sq[0:r, j % 2].rearrange("p (h c) -> p h c", h=HG),
                                         AX_X).then_inc(k_step, 1)
                    dve.wait_ge(k_step, base + 1)
                    nc.vector.tensor_scalar(ss_k[:, j % 2], ss_k[:, j % 2], 1.0 / NOPE, EPS, ALU.mult,
                                            ALU.add).then_inc(k_step, 1)
                    dve.wait_ge(k_step, base + 2)
                    nc.vector.reciprocal(ss_k[:, j % 2], ss_k[:, j % 2]).then_inc(k_step, 1)
                    if j >= 1:
                        norm_keys(j - 1)
                    if j >= 9:
                        take_queries(j - 9)
                norm_keys(KT_N - 1)
                take_queries(NT - 1)

                for step, n in ORDER:
                    if step == "score":
                        kind, a, blk = ITEMS[n]
                        dve.wait_ge(scored, g * NI + (n + 1))
                        if kind == "prompt":
                            s = ps[:, (4 * a + blk) % 2, 0:(blk + 1) * P]
                        else:
                            s = ps[:, 2:5, :].rearrange("p b c -> p (b c)")[:, 0:SKEYS]
                        nc.vector.reduce_max(neg_max[:, n:n + 1], s, AX_X, negate=True).then_inc(max_set, 1)
                    elif step == "turn" and n % 2:
                        take_piece(dve, nc.vector.tensor_copy, n, g, piece_odd)
                    elif step == "pv":
                        item = PIECES[n][0]
                        if n != NP - 1 and out_of(PIECES[n + 1][0]) == out_of(item):
                            continue
                        kind, a, blk = ITEMS[item]
                        o = out_of(item)
                        i0 = item - 3 if kind == "prompt" else item
                        dve.wait_ge(probs_set, g * NI + (item + 1))
                        nc.vector.reciprocal(inv_sums[:, i0:item + 1], sums[:, i0:item + 1]).then_inc(inv_sums_set, 1)
                        dve.wait_ge(inv_sums_set, g * NO + (o + 1))
                        dve.wait_ge(pv_done, g * NP + (n + 1))
                        if kind == "prompt":
                            at = (a % 2) * VD
                            nc.vector.tensor_tensor(
                                o_tok[:, a // 2, 0:4, at:at + VD],
                                ps[:, 7, 0:4 * VD].rearrange("p (b c) -> p b c", b=4),
                                inv_sums[:, i0:item + 1].unsqueeze(2).broadcast_to([P, 4, VD]),
                                ALU.mult).then_inc(o_read, 1)
                        else:
                            nc.vector.tensor_scalar(o_tok[0:DEC, a, 4, 0:VD], ps[0:DEC, 7, 0:VD],
                                                    inv_sums[0:DEC, item:item + 1], None, ALU.mult)
                            nc.vector.tensor_scalar(o_tok[0:DEC, a, 4, VD:2 * VD], ps[DEC:2 * DEC, 7, 0:VD],
                                                    inv_sums[DEC:2 * DEC, item:item + 1], None,
                                                    ALU.mult).then_inc(o_read, 1)
                    elif step == "gather":
                        kt = g * 2 + n
                        dve.wait_ge(hid_hi_set, kt + (B_O + 1))
                        nc.vector.tensor_tensor(hid_lo[:, ds(kt, 1), 0:SEQ], ps[:, 2:3, :],
                                                hid_hi[:, ds(kt, 1), 0:SEQ].bitcast(F32), ALU.subtract)
                        nc.vector.tensor_tensor(hid_lo[:, ds(kt, 1), SEQ:T], ps[:, 3:4, 0:DEC],
                                                hid_hi[:, ds(kt, 1), SEQ:T].bitcast(F32),
                                                ALU.subtract).then_inc(hid_ready, 1)

            project_back(F_O, U_O, last_s=3)
            mlp(F_MLP1, U_MLP1, B_MLP1, 3, 2, None)

        @block.scalar
        def _(act):
            for k in range(KD):
                act.dma_start(x[:, k, :], xt[:, k, :]).then_inc(x_loaded[k], 16)
            for dst, src in ((gains_sb[:], gains), (sgu_g[:], sgu_gcol),
                             (v_out[:], sgu_grow.partition_broadcast(DEC)),
                             (gq_row[:], q_rope_g.partition_broadcast(P)),
                             (gq_col[0:NOPE, :], q_nope_g), (gk_col[0:NOPE, :], k_nope_g),
                             (cs_sb[:], rope_cs)):
                act.dma_start(dst, src).then_inc(const_loaded, 16)

            def load_half(half):
                at = slice(8 * half, 8 * half + 8)
                act.dma_start(ws_sb[0:CHUNK, :, :], ws[0:CHUNK, at, :]).then_inc(half_loaded, 16)
                act.dma_start(ws_sb[CHUNK:P, :, CHUNK:P], ws[CHUNK:P, at, CHUNK:P]).then_inc(half_loaded, 16)
                act.dma_start(b_bc[:], bs[at, :].partition_broadcast(P)).then_inc(half_loaded, 16)

            load_half(0)

            def operand_and_square(m, slot, s):
                nc.scalar.activation(h_hi[:, ds(m, 1), :], x[:, ds(m, 1), :], ACT.Copy,
                                     scale=gains_sb[:, s, ds(m, 1)]).then_inc(h_hi_set, 1)
                nc.scalar.activation(act_t[:, slot, :].unsqueeze(1), x[:, ds(m, 1), :], ACT.Square).then_inc(x_sq, 1)

            def norm_root(s):
                act.wait_ge(inv_set, s + 1)
                nc.scalar.activation(rms_tok[:], inv_tok[:], ACT.Sqrt).then_inc(rms_set, 1)

            def norm_take(n):
                act.wait_ge(rms_spread, n + 1)
                nc.scalar.copy(rms_bc[:, 0:SEQ], ps[:, 5, :]).then_inc(rms_bc_set, 1)
                nc.scalar.copy(rms_bc[:, SEQ:T], ps[:, 6, 0:DEC]).then_inc(rms_bc_set, 1)

            act.wait_ge(const_loaded, 16 * CONSTS)
            for k in range(KD):
                act.wait_ge(x_loaded[k], 16)
                if k >= 2:
                    act.wait_ge(sq_added, k)
                operand_and_square(k, k % 2, 0)
            norm_root(0)
            norm_take(0)

            act.wait_ge(rms_set, 1)
            act.wait_ge(set_up, SETUPS)
            with act.Fori(0, 2, 1) as c2:
                for parity in range(2):
                    c = c2 * 2 + parity
                    for t in range(NT):
                        r = ROWS[t]
                        if t < NT - 1:
                            act.wait_ge(tok_done, c * 4 + (t + 1))
                        else:
                            act.wait_ge(unit_done, c * 4 + 4)
                        vc = v[0:r, t, ds(c * 512, 512)]
                        nc.scalar.activation(vc, ps[0:r, bank_of(parity, t), :], ACT.Gelu,
                                             scale=rms_tok[0:r, t:t + 1]).then_inc(tok_read, 1)
                        act.wait_ge(tok_read, c * 5 + (10 + t + 1))
                        nc.scalar.activation(junk[0:r, :], vc, ACT.Square,
                                             accum_out=ss_v[0:r, t, ds(c, 1)]).then_inc(ss_v_set, 1)
            act.wait_ge(rms_v_step, 3)
            nc.scalar.activation(rms_v[:], ss_v1[:], ACT.Sqrt).then_inc(rms_v_set, 1)

            def gate(half):
                with act.Fori(0, 2, 1) as i:
                    for u in range(4):
                        m = i * 4 + u
                        g = i * 4 + (half * 8 + u)
                        act.wait_ge(tile_read, i * 4 + (half * 16 + u + 3))
                        nc.scalar.activation(act_t[:, u % 2, :], act_t[:, u % 2, :], ACT.Gelu).then_inc(u_set, 1)
                        act.wait_ge(y_set, g + 1)
                        nc.scalar.copy(hid_hi[:, ds(m, 1), :], mixed[:].unsqueeze(1)).then_inc(hid_hi_set, 1)

            def operands(s, f0):
                with act.Fori(0, 2, 1) as i:
                    for u in range(4):
                        m = i * 4 + u
                        act.wait_ge(tile_read, m + (f0 + 3))
                        operand_and_square(m, u % 2, s)

            gate(0)
            act.wait_ge(mix_read, 4 + 16)
            load_half(1)
            act.wait_ge(v_out_set, 1)
            act.dma_start(out_v, v_out[:]).then_inc(stored, 16)
            gate(1)
            operands(1, 24)

            def mlp(f0, b0, n_sq, s, spread_n, last_s):
                norm_root(s)
                norm_take(spread_n)
                with act.Fori(0, 4, 1) as q:
                    with act.Fori(0, 2, 1) as i:
                        for u in range(4):
                            m = i * 4 + u
                            act.wait_ge(tile_read, q * 16 + m + (f0 + 3))
                            nc.scalar.activation(act_t[:, u % 2, :], act_t[:, u % 2, :],
                                                 ACT.Square).then_inc(hid_sq, 1)
                            act.wait_ge(hid_sq, q * 8 + m + (n_sq + 1))
                            nc.scalar.copy(hid_hi[:, ds(m, 1), :], act_t[:, u % 2, :].unsqueeze(1)).then_inc(
                                hid_hi_set, 1)
                if last_s is not None:
                    operands(last_s, f0 + 56)

            mlp(F_MLP0, B_MLP0, 0, 1, 1, 2)

            act.dma_start(cache_raw[:], cache_ct).then_inc(cache_loaded, 16)
            act.dma_start(lat_g_bc[:], lat_g.partition_broadcast(P)).then_inc(cache_loaded, 16)
            act.wait_ge(cache_loaded, 32)
            for k in range(2):
                nc.scalar.copy(cT_hi[:, k, SEQ:SEQ + PAST], cache_raw[:, k, :]).then_inc(cache_hi, 1)
            norm_root(2)
            act.wait_ge(rms_set, 3)
            act.wait_ge(set_up, SETUPS)
            parts = [(0, QL), (QL, KL), (QL + KL, ROPE)]
            for c in range(2):
                at, width = (0, QL) if c == 0 else (QL, KL + ROPE)
                for t in range(NT):
                    r = ROWS[t]
                    if t < NT - 1:
                        act.wait_ge(tok_done, 16 + 4 * c + t + 1)
                    else:
                        act.wait_ge(unit_done, U_IN + 4 * c + 4)
                    nc.scalar.activation(lat[0:r, t, at:at + width], ps[0:r, bank_of(c, t), 0:width], ACT.Copy,
                                         scale=rms_tok[0:r, t:t + 1]).then_inc(tok_read, 1)
                    act.wait_ge(tok_read, 30 + 5 * c + t + 1)
                    for w in ((0,), (1, 2))[c]:
                        a, n = parts[w]
                        nc.scalar.activation(junk[0:r, a - at:a - at + n], lat[0:r, t, a:a + n], ACT.Square,
                                             accum_out=ss_lat[0:r, w, t:t + 1]).then_inc(ss_lat_set, 1)
                if c == 0:
                    act.wait_ge(lat_step, 2)
                    nc.scalar.activation(rms_lat[:, 0, :], ss_lat[:, 0, :], ACT.Sqrt).then_inc(rms_lat_set, 1)
            act.wait_ge(unit_done, U_GRP)
            act.dma_start(kT[NOPE:QK, :, SEQ:SEQ + PAST],
                          cache_krt.unsqueeze(1).broadcast_to([ROPE, HG, PAST])).then_inc(rows_loaded, 16)
            act.dma_start(kT[QK:QK + 1, :, 0:SEQ], mask_rows[0:1]).then_inc(rows_loaded, 16)
            act.dma_start(qT[QK:QK + 1, :, 0:SEQ], mask_rows[1:2]).then_inc(rows_loaded, 16)
            act.wait_ge(lat_step, 5)
            nc.scalar.activation(rms_lat[:, 1:3, :], ss_lat[:, 1:3, :], ACT.Sqrt).then_inc(rms_lat_set, 1)
            for L in range(2 * NT):
                t = L % NT
                r = ROWS[t]
                hi, lo, at = latent_target(L)
                n_k = 3 if L < NT else 2
                act.wait_ge(lat_turned, L + 1)
                nc.scalar.copy(hi[:, :, at:at + r],
                               ps[:, 2 + L % 3, 0:n_k * P].rearrange("p (k c) -> p k c", k=n_k)[:, :, 0:r]).then_inc(
                    lat_hi, 1)
            act.wait_ge(kr_turned, 1)
            nc.scalar.copy(kT[NOPE:QK, :, 0:SEQ], ps[NOPE:QK, 0:1, :].broadcast_to([ROPE, HG, SEQ])).then_inc(kr_set, 1)
            act.wait_ge(kr_turned, 2)
            nc.scalar.copy(kT[NOPE:QK, :, SEQ + PAST:KEYS],
                           ps[NOPE:QK, 1:2, 0:DEC].broadcast_to([ROPE, HG, DEC])).then_inc(kr_set, 1)
            act.wait_ge(lat_ready, 3 * NT)
            act.wait_ge(krr_step, 9)
            act.dma_start(out_kv[0:SEQ, :].rearrange("(t p) c -> p t c", p=P),
                          lat[:, 0:4, QL:QL + KL]).then_inc(stored, 16)
            act.dma_start(out_kv[SEQ:T, :], lat[0:DEC, 4, QL:QL + KL]).then_inc(stored, 16)
            act.dma_start(out_kr[0:SEQ, :].rearrange("(t p) c -> p t c", p=P),
                          krr[:, 0:4, NOPE:QK]).then_inc(stored, 16)
            act.dma_start(out_kr[SEQ:T, :], krr[0:DEC, 4, NOPE:QK]).then_inc(stored, 16)

            with act.Fori(0, NG, 1) as g:
                for t in range(NT):
                    r = ROWS[t]
                    if t < NT - 1:
                        act.wait_ge(q_done, g * (NT - 1) + (t + 1))
                    else:
                        act.wait_ge(unit_done, g * 4 + (U_GRP + 3))
                    if t >= 2:
                        act.wait_ge(q_read, g * NT + (t - 1))
                    nc.scalar.activation(q_sq[0:r, t % 2, :], ps[0:r, t, 0:HG * QK], ACT.Square).then_inc(q_sq_set, 1)

                def key_root(j):
                    act.wait_ge(k_step, g * (3 * KT_N) + (3 * j + 3))
                    nc.scalar.activation(rms_k[:, j % 2], ss_k[:, j % 2], ACT.Sqrt).then_inc(rms_k_set, 1)

                def take_keys(j):
                    r = key_rows(j)
                    act.wait_ge(k_turned, g * KT_N + (j + 1))
                    nc.scalar.copy(kT[0:NOPE, :, key_at(j):key_at(j) + r],
                                   ps[0:NOPE, 2 + j % 2, :].rearrange("p (h c) -> p h c", h=HG)[:, :, 0:r]).then_inc(
                        kT_set, 1)

                for j in range(KT_N):
                    r = key_rows(j)
                    b = 5 + j % 3
                    if j < KT_N - 1:
                        act.wait_ge(kv_done, g * (KT_N - 1) + (j + 1))
                    else:
                        act.wait_ge(unit_done, g * 4 + (U_GRP + 4))
                    if j >= 2:
                        act.wait_ge(k_step, g * (3 * KT_N) + (3 * (j - 2) + 1))
                    nc.scalar.activation(k_sq[0:r, j % 2, :], ps[0:r, b, 0:HG * NOPE], ACT.Square).then_inc(k_sq_set, 1)
                    nc.scalar.copy(vals[0:r, j, :], ps[0:r, b, HG * NOPE:512]).then_inc(vals_set, 1)
                    if j == 2:
                        act.wait_ge(q_step_d, g * 9 + 9)
                        nc.scalar.activation(rms_q[:], ss_q[:], ACT.Sqrt).then_inc(rms_q_set, 1)
                    if j >= 1:
                        key_root(j - 1)
                    if j >= 3:
                        take_keys(j - 3)
                key_root(KT_N - 1)
                take_keys(KT_N - 3)

                for step, n in ORDER:
                    if step == "score":
                        kind, a, blk = ITEMS[n]
                        act.wait_ge(max_set, g * NI + (n + 1))
                        same = [x for x in range(n) if ITEMS[x][0] == kind]
                        back = 2 if kind == "prompt" else 1
                        if len(same) >= back:
                            act.wait_ge(piece_turned, g * NP + (PIECES_OF[same[-back]][-1] + 1))
                        if kind == "prompt":
                            w = (blk + 1) * P
                            dst, src = probs[:, (4 * a + blk) % 2, 0:w], ps[:, (4 * a + blk) % 2, 0:w]
                        else:
                            dst = probs_s[:]
                            src = ps[:, 2:5, :].rearrange("p b c -> p (b c)")[:, 0:SKEYS]
                        nc.scalar.activation(dst, src, ACT.Exp, bias=neg_max[:, n:n + 1],
                                             accum_out=sums[:, n:n + 1]).then_inc(probs_set, 1)
                    elif step == "key":
                        take_keys(n)
                    elif step == "turn" and n % 2 == 0:
                        take_piece(act, nc.scalar.copy, n, g, piece_even)
                    elif step == "gather":
                        kt = g * 2 + n
                        act.wait_ge(stored, 16 * 5)
                        act.wait_ge(o_gathered, g * 4 + (2 * n + 2))
                        nc.scalar.copy(hid_hi[:, ds(kt, 1), 0:SEQ], ps[:, 2:3, :])
                        nc.scalar.copy(hid_hi[:, ds(kt, 1), SEQ:T], ps[:, 3:4, 0:DEC]).then_inc(hid_hi_set, 1)

            operands(3, F_O)
            mlp(F_MLP1, B_MLP1, 32, 3, 2, None)
            with act.Fori(0, KD, 1) as m:
                act.wait_ge(tile_read, m + (F_MLP1 + 56 + 3))
                act.dma_start(out_x[:, ds(m, 1), :], x[:, ds(m, 1), :]).then_inc(stored, 16)
            act.wait_ge(stored, 16 * (5 + KD))


def _units(*blocks):
    out = []
    for w, k_tiles, pitch in blocks:
        u = np.zeros((P, UNIT), np.float32)
        for k in range(k_tiles):
            u[:, k * pitch:k * pitch + w.shape[1]] = w[k * P:(k + 1) * P]
        out.append(u)
    return out


def _feature_major(w, rows, n_tiles):
    return _units(*[(w[rows:rows + 8 * P, m * P:(m + 1) * P], 8, P) for m in range(n_tiles)])


def _weight_stream(sgu_in, sgu_out, up, down, mla_in, uq, ukv, wo):
    units = []
    v_part = sgu_in[:, DS:]
    for c in range(4):
        units += _units(*[(v_part[2 * j * P:2 * (j + 1) * P, c * 512:(c + 1) * 512], 2, 512) for j in range(4)])
    for half in range(2):
        units += _feature_major(sgu_in[:, half * D:(half + 1) * D], 0, 8)
        units += _feature_major(sgu_out, half * D, 8)

    def mlp(layer):
        out = []
        for q in range(4):
            out += _feature_major(up[layer][:, q * D:(q + 1) * D], 0, 8)
            out += _feature_major(down[layer], q * D, 8)
        return out

    units += mlp(0)
    for lo, hi in ((0, QL), (QL, QL + KL + ROPE)):
        units += _units(*[(mla_in[2 * j * P:2 * (j + 1) * P, lo:hi], 2, 512) for j in range(4)])
    kv = ukv.reshape(KL, HEADS, NOPE + VD)
    for g in range(NG):
        heads = slice(g * HG, (g + 1) * HG)
        q_cols = uq[:, g * HG * QK:(g + 1) * HG * QK]
        units += _units(*[(q_cols[k * P:(k + 1) * P], 1, 512) for k in range(3)])
        both = np.concatenate([kv[:, heads, :NOPE].reshape(KL, -1), kv[:, heads, NOPE:].reshape(KL, -1)], 1)
        units += _units((both, 2, 512))
    units += _feature_major(wo, 0, 8)
    units += mlp(1)
    assert len(units) == UNITS
    return np.stack(units)


def _rope_tables():
    half = ROPE // 2
    inv = (np.float32(10000.0) ** (-np.arange(half, dtype=np.float32) / np.float32(half))).astype(np.float32)
    pos = np.concatenate([np.arange(SEQ), PAST + np.arange(DEC)]).astype(np.float32)
    ang = (pos[:, None] * inv[None, :]).astype(np.float32)
    cos, sin = np.cos(ang), np.sin(ang)
    table = np.zeros((P, 2, NT, ROPE), np.float32)
    for t in range(NT):
        r = ROWS[t]
        at = slice(t * P, t * P + r)
        table[:r, 0, t] = np.concatenate([cos[at], cos[at]], 1)
        table[:r, 1, t] = np.concatenate([-sin[at], sin[at]], 1)
    return table


def _mask_rows():
    odd = (np.arange(SEQ) // CHUNK) % 2 == 1
    rows = np.zeros((2, HG, SEQ), np.float32)
    rows[0, :, odd] = MASKED
    rows[1, :, ~odd] = 1.0
    return rows


def kernel(**inputs):
    import concourse.bacc as _bacc
    from concourse.bass_utils import run_bass_kernel_spmd as _run

    a = {k: np.asarray(w) for k, w in inputs.items()}
    tokens = np.concatenate([a["x_prompt"][0], a["x_sample"][0]], 0)
    arrays = {
        "xt": tokens.T.reshape(KD, P, T).transpose(1, 0, 2),
        "gains": np.stack([a["mix_norm_g"][0], a["mlp_norm_g"][0], a["mix_norm_g"][1], a["mlp_norm_g"][1]])
                   .reshape(4, KD, P).transpose(2, 0, 1),
        "stream": _weight_stream(a["sgu_w_in"][0], a["sgu_w_out"][0], a["mlp_w_up"], a["mlp_w_down"],
                                 a["mla_w_in"][0], a["mla_w_uq"][0], a["mla_w_ukv"][0], a["mla_w_o"][0]),
        "ws": a["sgu_w_s"][0].transpose(2, 0, 1),
        "bs": a["sgu_b_s"][0],
        "sgu_gcol": a["sgu_norm_g"][0].reshape(GROUPS, P).T,
        "sgu_grow": a["sgu_norm_g"][0],
        "cache_ct": a["cache_kv_latent"][0, 0].T.reshape(2, P, PAST).transpose(1, 0, 2),
        "cache_krt": a["cache_k_rope"][0, 0].T,
        "lat_g": np.concatenate([a["mla_q_norm_g"][0], a["mla_kv_norm_g"][0], a["mla_k_rope_g"][0]]),
        "q_nope_g": a["mla_q_nope_g"][0][:, None],
        "q_rope_g": a["mla_q_rope_g"][0],
        "k_nope_g": a["mla_k_nope_g"][0][:, None],
        "rope_cs": _rope_tables(),
        "mask_rows": _mask_rows(),
    }
    outs = {"out_x": (P, KD, T), "out_kv": (T, KL), "out_kr": (T, ROPE), "out_v": (DEC, DS)}
    nc = _bacc.Bacc("TRN2", target_bir_lowering=False, num_devices=1, dynamic_dma_scratch_size=1024)
    args = {}
    for name, value in arrays.items():
        arrays[name] = value = np.ascontiguousarray(value)
        args[name] = nc.dram_tensor(name, value.shape, mybir.dt.from_np(value.dtype), kind="ExternalInput").ap()
    for name, shape in outs.items():
        args[name] = nc.dram_tensor(name, shape, F32, kind="ExternalOutput").ap()
    build_trunk(nc, **args)
    r = _run(nc, [arrays], core_ids=[0]).results[0]
    y = r["out_x"].transpose(1, 0, 2).reshape(D, T).T
    kv, kr = r["out_kv"], r["out_kr"]
    return (y[None, :SEQ], y[None, SEQ:], kv[None, None, :SEQ], kr[None, None, :SEQ], kv[None, None, SEQ:],
            kr[None, None, SEQ:], r["out_v"][None, None])
```

```python
from contextlib import ExitStack

import numpy as np

import concourse.bass as bass
from concourse import mybir

F32 = mybir.dt.float32
F32R = mybir.dt.float32r
ALU = mybir.AluOpType
ACT = mybir.ActivationFunctionType
AX_X = mybir.AxisListType.X

P = 128
D = 1024
KD = D // P
SEQ, DEC, PAST = 512, 64, 1024
T = SEQ + DEC
TH = T // 2
NT = 5
ROWS = [P] * 4 + [DEC]
CHUNK = 64
DS = 2 * D
GROUPS = DS // P
DFF = 4 * D
HEADS, NOPE, ROPE, VD = 16, 64, 32, 64
QK = NOPE + ROPE
QL, KL = 384, 256
KEYS = SEQ + PAST + DEC
KT_N = 13
SKEYS = PAST + DEC
EPS = 1e-6
MASKED = -1e30
SCALE = 1.0 / float(QK) ** 0.5

HG = 4
NG = HEADS // HG
UNIT = 1024
SLOTS = 4
SCRATCH = 26112

U_V = 0
U_SGU = 16
U_MLP0 = 48
U_IN = 112
U_GRP = 120
U_O = 136
U_MLP1 = 144
UNITS = 208
F_SGU, F_MLP0, F_O, F_MLP1 = 0, 32, 96, 104
B_SGU, B_MLP0, B_O, B_MLP1 = 0, 16, 48, 56

PROMPT = [("prompt", h, b) for h in range(HG) for b in range(4)]
ITEMS = PROMPT[:3] + [("sample", 0, 0), ("sample", 1, 0)] + PROMPT[3:]
NI = len(ITEMS)
SAMPLE_ITEM = 3
PIECES = []
for _h in range(HG):
    for _b in range(4):
        PIECES.append((ITEMS.index(("prompt", _h, _b)), list(range(_b + 1))))
        if _h % 2 and _b < 3:
            PIECES.append((ITEMS.index(("sample", _h // 2, 0)), list(range(3 * _b, 3 * _b + 3))))
NP = len(PIECES)
EVEN_PIECES = (NP + 1) // 2
RING = 3
SCORE_BANK, PIECE_BANK, OUT_BANK = 0, 3, 6
OUTS = [("prompt", 0), ("sample", 0), ("prompt", 1), ("prompt", 2), ("sample", 1), ("prompt", 3)]
NO = len(OUTS)


def out_of(item):
    kind, a, _ = ITEMS[item]
    return OUTS.index((kind, a))


def stat_of(item):
    kind, a, blk = ITEMS[item]
    return 4 * a + blk if kind == "prompt" else 4 * HG + a


def attention_order():
    steps = [("key", KT_N - 3), ("score", 0), ("score", 1), ("key", KT_N - 2), ("score", 2), ("key", KT_N - 1),
             ("samples", 0)]
    steps += [("score", ITEMS.index(PROMPT[i])) for i in range(RING, 2 * RING)]
    owed = []
    for p, (item, _) in enumerate(PIECES):
        kind, a, blk = ITEMS[item]
        ahead = 4 * a + blk + 3
        if kind == "prompt" and 2 * RING <= ahead < len(PROMPT):
            steps.append(("score", ITEMS.index(PROMPT[ahead])))
        steps.append(("turn", p))
        owed.append(p)
        if len(owed) > 2:
            steps.append(("pv", owed.pop(0)))
        if (kind, a, blk) == ("prompt", 3, 1):
            steps.append(("gather", 0))
    return steps + [("pv", p) for p in owed]


ORDER = attention_order()
ACT_ORDER = []
_late = []
for _step in ORDER:
    if _step[0] == "score":
        _late.append(_step)
        continue
    if _step[0] == "samples":
        ACT_ORDER += _late
        _late = []
    ACT_ORDER.append(_step)
    if _step[0] == "turn" and _late:
        ACT_ORDER.append(_late.pop(0))


def score_banks():
    at, used, plan = 0, {}, {}
    for step in ORDER:
        if step[0] == "score" or step == ("gather", 0):
            n = 1 if step[0] == "score" else 2
            banks = [SCORE_BANK + (at + i) % RING for i in range(n)]
            plan[step] = (banks, [used.get(b) for b in banks])
            used.update({b: step for b in banks})
            at += n
    return plan


SCORE_PLAN = score_banks()


def build_trunk(nc, xt, gains, stream, ws, bs, sgu_gcol, sgu_grow, cache_ct, cache_krt, lat_g, q_nope_g,
                q_rope_g, k_nope_g, rope_cs, mask_rows, out_x, out_kv, out_kr, out_v):
    with ExitStack() as ctx:
        sem_of = lambda name: ctx.enter_context(nc.semaphore(name))

        cursor = [0]

        def region(size):
            at = cursor[0]
            cursor[0] += (size + 31) // 32 * 32
            return at

        base0 = nc.sbuf_base
        cursor[0] = (base0 + 31) // 32 * 32

        def place(name, shape, dt, at):
            return nc.alloc_sbuf_tensor_at(name, shape, dt, offset=at)

        def new(name, shape, dt=F32):
            return place(name, shape, dt, region(4 * int(np.prod(shape[1:]))))

        x = new("x", [P, KD, T])
        a_at = region(2 * 4 * KD * T)
        h_hi = place("h_hi", [P, KD, T], F32R, a_at)
        h_lo = place("h_lo", [P, KD, T], F32R, a_at + 4 * KD * T)
        kT = place("kT", [P, HG, KEYS], F32, a_at)
        qT = place("qT", [P, HG, T], F32, a_at + 4 * HG * KEYS)
        b_at = region(2 * 4 * KD * T)
        hid_hi = place("hid_hi", [P, KD, T], F32R, b_at)
        hid_lo = place("hid_lo", [P, KD, T], F32R, b_at + 4 * KD * T)
        lat = place("lat", [P, NT, QL + KL + ROPE], F32, b_at)
        LAT = QL + KL + ROPE
        lat_g_bc = place("lat_g_bc", [P, LAT], F32, b_at + 4 * NT * LAT)
        krr = place("krr", [P, NT, QK], F32, b_at + 4 * (NT + 1) * LAT)
        raw = new("raw", [P, SLOTS, UNIT])
        w_hi = new("w_hi", [P, SLOTS, UNIT], F32R)
        w_lo = new("w_lo", [P, SLOTS, UNIT], F32R)
        v_at = region(4 * NT * DS)
        v = place("v", [P, NT, DS], F32, v_at)
        cT_hi = place("cT_hi", [P, 2, KEYS], F32R, v_at)
        cT_lo = place("cT_lo", [P, 2, KEYS], F32R, v_at + 8 * KEYS)
        cqT_hi = place("cqT_hi", [P, 3, T], F32R, v_at + 16 * KEYS)
        cqT_lo = place("cqT_lo", [P, 3, T], F32R, v_at + 16 * KEYS + 12 * T)
        s_at = region(4 * KT_N * HG * VD)
        ws_sb = place("ws_sb", [P, 8, P], F32, s_at)
        b_bc = place("b_bc", [P, 8, P], F32, s_at + 4096)
        vn = place("vn", [P, 2, NT, P], F32, s_at + 8192)
        cache_raw = place("cache_raw", [P, 2, PAST], F32, s_at)
        vals = place("vals", [P, KT_N, HG * VD], F32, s_at)
        r_at = region(SCRATCH)
        bump = [r_at]

        def scratch(name, shape, dt=F32):
            at = bump[0]
            bump[0] += (4 * int(np.prod(shape[1:])) + 31) // 32 * 32
            assert bump[0] <= r_at + SCRATCH, name
            return place(name, shape, dt, at)

        rms_bc = scratch("rms_bc", [P, T])
        sq_sum = scratch("sq_sum", [P, T])
        act_t = scratch("act_t", [P, 2, T])
        mixed = scratch("mixed", [P, T])
        diag = scratch("diag", [P, NT, P])
        v_out = scratch("v_out", [DEC, DS])
        junk = scratch("junk", [P, 512])
        bump[0] = r_at
        q_tok = scratch("q_tok", [P, NT, HG, QK])
        rope_a = scratch("rope_a", [P, NT, HG, ROPE])
        rope_b = scratch("rope_b", [P, NT, HG, ROPE])
        k_sq = scratch("k_sq", [P, 2, HG * NOPE])
        q_sq = scratch("q_sq", [P, 2, HG * QK])
        k_norm = scratch("k_norm", [P, 3, HG, NOPE])
        bump[0] = r_at
        probs = scratch("probs", [P, RING, SEQ])
        probs_s = scratch("probs_s", [P, 2, SKEYS])
        turned = scratch("turned", [P, RING, SEQ])
        o_tok = scratch("o_tok", [P, 2, NT, P])
        ident = new("ident", [P, P])
        ones = new("ones", [P, P])
        gains_sb = new("gains_sb", [P, 4, KD])
        sgu_g = new("sgu_g", [P, GROUPS])
        gq_row = new("gq_row", [P, ROPE])
        gq_col = new("gq_col", [P, 1])
        gk_col = new("gk_col", [P, 1])
        cs_q = new("cs_q", [P, 2, NT, ROPE])
        cs_sb = new("cs_sb", [P, 2, NT, ROPE])
        var_tok = new("var_tok", [P, NT])
        inv_tok = new("inv_tok", [P, NT])
        rms_tok = new("rms_tok", [P, NT])
        ss_v = new("ss_v", [P, NT, 4])
        ss_v1 = new("ss_v1", [P, NT])
        rms_v = new("rms_v", [P, NT])
        ss_lat = new("ss_lat", [P, 3, NT])
        rms_lat = new("rms_lat", [P, 3, NT])
        ss_q = new("ss_q", [P, NT, HG, 3])
        ss_q2 = new("ss_q2", [P, NT, HG])
        rms_q = new("rms_q", [P, NT, HG, 3])
        ss_k = new("ss_k", [P, 2, HG])
        rms_k = new("rms_k", [P, 2, HG])
        neg_max = new("neg_max", [P, NI])
        sums = new("sums", [P, NI])
        inv_sums = new("inv_sums", [P, NI])
        assert cursor[0] <= nc.sbuf_usable_end, (cursor[0], nc.sbuf_usable_end)

        ps = ctx.enter_context(nc.psum_tensor("ps", [P, 8, 512], F32))

        x_loaded = [sem_of(f"x_loaded{k}") for k in range(KD)]
        gains_loaded = sem_of("gains_loaded")
        const_loaded = sem_of("const_loaded")
        half_loaded = sem_of("half_loaded")
        cache_loaded = sem_of("cache_loaded")
        rows_loaded = sem_of("rows_loaded")
        stored = sem_of("stored")
        raw_loaded = [sem_of(f"raw_loaded{i}") for i in range(SLOTS)]
        split_hi = sem_of("split_hi")
        split_lo = sem_of("split_lo")
        unit_done = sem_of("unit_done")
        ones_set = sem_of("ones_set")
        set_up = sem_of("set_up")
        ident_zero = sem_of("ident_zero")
        ident_set = sem_of("ident_set")
        tile_read = sem_of("tile_read")
        h_hi_set = sem_of("h_hi_set")
        h_ready = sem_of("h_ready")
        x_sq = sem_of("x_sq")
        sq_added = sem_of("sq_added")
        stat_summed = sem_of("stat_summed")
        var_set = sem_of("var_set")
        inv_set = sem_of("inv_set")
        rms_set = sem_of("rms_set")
        diag_set = sem_of("diag_set")
        rms_spread = sem_of("rms_spread")
        rms_bc_set = sem_of("rms_bc_set")
        tok_done = sem_of("tok_done")
        tok_read = sem_of("tok_read")
        v_set = sem_of("v_set")
        ss_v_set = sem_of("ss_v_set")
        rms_v_step = sem_of("rms_v_step")
        rms_v_set = sem_of("rms_v_set")
        v_out_set = sem_of("v_out_set")
        vn_ready = sem_of("vn_ready")
        u_set = sem_of("u_set")
        mix_done = sem_of("mix_done")
        mix_read = sem_of("mix_read")
        y_set = sem_of("y_set")
        hid_sq = sem_of("hid_sq")
        hid_hi_set = sem_of("hid_hi_set")
        hid_ready = sem_of("hid_ready")
        cache_hi = sem_of("cache_hi")
        cache_split = sem_of("cache_split")
        ss_lat_set = sem_of("ss_lat_set")
        lat_step = sem_of("lat_step")
        rms_lat_set = sem_of("rms_lat_set")
        lat_ready = sem_of("lat_ready")
        krr_step = sem_of("krr_step")
        lat_turned = sem_of("lat_turned")
        lat_hi = sem_of("lat_hi")
        lat_split = sem_of("lat_split")
        kr_turned = sem_of("kr_turned")
        kr_set = sem_of("kr_set")
        gq_step = sem_of("gq_step")
        q_done = sem_of("q_done")
        q_sq_set = sem_of("q_sq_set")
        q_read = sem_of("q_read")
        q_step = sem_of("q_step")
        q_step_d = sem_of("q_step_d")
        rms_q_set = sem_of("rms_q_set")
        q_roped = sem_of("q_roped")
        q_ready = sem_of("q_ready")
        q_turned = sem_of("q_turned")
        qT_set = sem_of("qT_set")
        kv_done = sem_of("kv_done")
        k_sq_set = sem_of("k_sq_set")
        vals_set = sem_of("vals_set")
        ss_k_set = sem_of("ss_k_set")
        k_step = sem_of("k_step")
        rms_k_set = sem_of("rms_k_set")
        k_ready = sem_of("k_ready")
        k_turned = sem_of("k_turned")
        kT_set = sem_of("kT_set")
        scored = sem_of("scored")
        max_set = sem_of("max_set")
        probs_set = sem_of("probs_set")
        piece_turned = sem_of("piece_turned")
        piece_even = sem_of("piece_even")
        piece_odd = sem_of("piece_odd")
        pv_done = sem_of("pv_done")
        inv_sums_set = sem_of("inv_sums_set")
        o_read = sem_of("o_read")
        o_gathered = sem_of("o_gathered")

        ds = bass.ds
        TILE_BANKS = (2, 0)
        STAT = 7
        SETUPS = 6
        CONSTS = 6

        def halves(a):
            return a.rearrange("p (n c) -> p n c", n=2)

        def tile_psum(slot):
            b = TILE_BANKS[slot]
            return ps[:, b:b + 2, 0:TH]

        def cols(t):
            return slice(t * P, t * P + ROWS[t])

        def bank_of(chunk, t):
            return t - 3 if t >= 3 else 2 + 3 * (chunk % 2) + t

        def key_rows(j):
            return P if j < KT_N - 1 else DEC

        def key_at(j):
            return j * P


        def turns_behind(j):
            return {8: (0,), 9: (1,), 10: (2,), 11: (3, 4)}.get(j, ())

        def key_bank(j):
            return (7, 5, 6, 2)[j % 4]

        def sample_scores(pair):
            at = 3 * 512 if pair == 0 else 8 * 512 - SKEYS
            return ps[:].rearrange("p b c -> p (b c)")[:, at:at + SKEYS]

        def sample_at(pair, kt):
            if pair == 0:
                return kt * P
            return DEC + kt * P if kt < 8 else 0

        def latent_bank(L):
            return 2 + L % 3 if L < NT else 5 + (L - NT) % 3

        def out_bank(o):
            return OUT_BANK + o % 2

        def gather_psum(pair):
            banks = SCORE_PLAN[("gather", 0)][0] if pair == 0 else (5, 6)
            return ps[:, banks[0]:banks[0] + 1, :], ps[:, banks[1]:banks[1] + 1, 0:DEC]

        def latent_target(L):
            t = L % NT
            if L < NT:
                return cqT_hi, cqT_lo, t * P
            return cT_hi, cT_lo, (t * P if t < 4 else SEQ + PAST)

        def take_piece(eng, copy, p, g, piece_set):
            item, tiles = PIECES[p]
            w = len(tiles) * P
            eng.wait_ge(piece_turned, g * NP + (p + 1))
            if p >= RING:
                eng.wait_ge(pv_done, g * NP + (p - RING + 1))
            copy(turned[:, p % RING, 0:w], ps[:, PIECE_BANK + p % RING, 0:w]).then_inc(piece_set, 1)

        def piece_set(p):
            return piece_odd if p % 2 else piece_even

        def pieces_by(p):
            return NP - EVEN_PIECES if p % 2 else EVEN_PIECES

        block = ctx.enter_context(nc.Block())

        @block.sync
        def _(sp):
            for u in range(SLOTS):
                sp.dma_start(raw[:, u, :], stream[u]).then_inc(raw_loaded[u], 16)
                sp.dma_start(x[:, 2 * u + 1, :], xt[:, 2 * u + 1, :]).then_inc(x_loaded[2 * u + 1], 16)
            with sp.Fori(1, UNITS // SLOTS, 1) as i:
                for u in range(SLOTS):
                    sp.wait_ge(split_lo, (i - 1) * SLOTS + u + 1)
                    sp.dma_start(raw[:, u, :], stream[i * SLOTS + u]).then_inc(raw_loaded[u], 16)

        @block.gpsimd
        def _(pool):
            loads, units = pool.alloc_register("loads"), pool.alloc_register("units")
            nc.gpsimd.memset(ident[:], 0.0).then_inc(ident_zero, 1)
            nc.gpsimd.memset(ones[:], 1.0).then_inc(ones_set, 1)
            nc.gpsimd.memset(var_tok[:], 1.0).then_inc(set_up, 1)
            nc.gpsimd.memset(ss_v[:], 1.0).then_inc(set_up, 1)
            nc.gpsimd.memset(ss_lat[:], 1.0).then_inc(set_up, 1)
            nc.gpsimd.memset(ss_q[:], 1.0).then_inc(set_up, 1)
            nc.gpsimd.memset(ss_k[:], 1.0).then_inc(set_up, 1)
            pool.wait_ge(ident_zero, 1)
            nc.gpsimd.affine_select(out=ident[:], in_=ident[:], compare_op=ALU.not_equal, fill=1.0, base=0,
                                    pattern=[[-1, P]], channel_multiplier=1).then_inc(ident_set, 1)

            def split(u, n, i, first=False):
                if not first:
                    pool.reg_mov(loads, i * 16 + 16)
                    pool.reg_mov(units, n - SLOTS + 1)
                    pool.wait_ge(ident_zero, 1)
                    pool.wait_ge(unit_done, units)
                pool.wait_ge(raw_loaded[u], 16 if first else loads)
                nc.gpsimd.tensor_scalar(w_hi[:, u, :], raw[:, u, :], 1.0, 0.0, ALU.mult, ALU.add).then_inc(split_hi, 1)
                pool.wait_ge(split_hi, n + 1)
                nc.gpsimd.tensor_tensor(w_lo[:, u, :], raw[:, u, :], w_hi[:, u, :].bitcast(F32),
                                        ALU.subtract).then_inc(split_lo, 1)

            for u in range(SLOTS):
                split(u, u, 0, first=True)
            with pool.Fori(1, (U_GRP + SLOTS) // SLOTS, 1) as i:
                for u in range(SLOTS):
                    split(u, i * SLOTS + u, i)

            def rope_products(tiles, rows):
                n = tiles.stop - tiles.start
                part = q_tok[0:rows, tiles, :, NOPE:QK]
                a, b = rope_a[0:rows, tiles], rope_b[0:rows, tiles]

                def table(which, lo, hi):
                    return cs_q[0:rows, which, tiles, lo:hi].unsqueeze(2).broadcast_to([rows, n, HG, hi - lo])

                h = ROPE // 2
                nc.gpsimd.tensor_tensor(a, part, table(0, 0, ROPE), ALU.mult).then_inc(q_step, 1)
                nc.gpsimd.tensor_tensor(b[:, :, :, 0:h], part[:, :, :, h:ROPE], table(1, 0, h),
                                        ALU.mult).then_inc(q_step, 1)
                nc.gpsimd.tensor_tensor(b[:, :, :, h:ROPE], part[:, :, :, 0:h], table(1, h, ROPE),
                                        ALU.mult).then_inc(q_step, 1)

            with pool.Fori(0, NG, 1) as g:
                pool.wait_ge(q_read, g * NT + NT)
                pool.wait_ge(rms_q_set, g + 1)
                for t in range(NT):
                    r = ROWS[t]
                    q3 = q_tok[0:r, t].rearrange("p h (s c) -> p (h s) c", c=ROPE)
                    w3 = rms_q[0:r, t].rearrange("p h s -> p (h s)").unsqueeze(2).broadcast_to([r, 3 * HG, ROPE])
                    nc.gpsimd.tensor_tensor(q3, q3, w3, ALU.mult).then_inc(q_step, 1)
                pool.wait_ge(q_step, g * 11 + 5)
                for steps, tiles, rows in ((8, slice(0, 4), P), (11, slice(4, 5), DEC)):
                    rope_products(tiles, rows)
                    pool.wait_ge(q_step, g * 11 + steps)
                    nc.gpsimd.tensor_tensor(q_tok[0:rows, tiles, :, NOPE:QK], rope_a[0:rows, tiles],
                                            rope_b[0:rows, tiles], ALU.add).then_inc(q_ready, 1)
                for u in range(SLOTS):
                    split(u, g * SLOTS + (U_GRP + SLOTS + u), g + (U_GRP + SLOTS) // SLOTS)
            with pool.Fori(U_O // SLOTS + 1, UNITS // SLOTS, 1) as i:
                for u in range(SLOTS):
                    split(u, i * SLOTS + u, i)

        @block.tensor
        def _(pe):
            filled, freed = pe.alloc_register("filled"), pe.alloc_register("freed")
            def three(out, l_hi, l_lo, r_hi, r_lo, first, last):
                nc.tensor.matmul(out, l_hi, r_hi, start=first, stop=False)
                nc.tensor.matmul(out, l_hi, r_lo, start=False, stop=False)
                return nc.tensor.matmul(out, l_lo, r_hi, start=False, stop=last)

            def feature_tile(u, f, n, operand, ready, count, middle=None):
                pe.wait_ge(split_lo, n + 1)
                pe.wait_ge(tile_read, f + 1)
                pe.wait_ge(ready, count - 1)
                o_hi, o_lo = operand
                for k in range(KD):
                    if k == KD - 1:
                        pe.wait_ge(ready, count)
                    if k == KD // 2 and middle:
                        middle()
                    for n2 in range(2):
                        tok = slice(n2 * TH, n2 * TH + TH)
                        last = three(tile_psum(u % 2)[:, n2, :], w_hi[:, u, k * P:(k + 1) * P],
                                     w_lo[:, u, k * P:(k + 1) * P], o_hi[:, k, tok], o_lo[:, k, tok],
                                     k == 0, k == KD - 1)
                last.then_inc(unit_done, 1)

            H = (h_hi, h_lo)
            HID = (hid_hi, hid_lo)

            def norm_sums(s):
                pe.wait_ge(sq_added, 9 * s + 9)
                for t in range(NT):
                    last = nc.tensor.matmul(ps[0:ROWS[t], STAT, t:t + 1], sq_sum[:, cols(t)], ones[:, 0:1],
                                            start=True, stop=True)
                last.then_inc(stat_summed, 1)

            def norm_spread(n):
                pe.wait_ge(diag_set, n + 1)
                for t in range(NT):
                    r = ROWS[t]
                    out = ps[:, 5, t * P:(t + 1) * P] if t < 4 else ps[:, 6, 0:DEC]
                    last = nc.tensor.matmul(out, ones[0:r, :], diag[0:r, t, 0:r], start=True, stop=True)
                last.then_inc(rms_spread, 1)

            def token_chunk(chunk, parity, first_unit, width, between=None, h_count=None, tiles=None):
                for j in range(4):
                    pe.wait_ge(split_lo, first_unit + j + 1)
                    if h_count is not None:
                        pe.wait_ge(h_ready, h_count + 2 * j + 2)
                    for t in range(NT):
                        if j == 0:
                            pe.wait_ge(tok_read, chunk * 5 + t + (1 if t < 3 else 6))
                            if tiles is not None and t in (0, 3):
                                pe.wait_ge(tile_read, tiles + (1 if t == 0 else 2))
                        for k2 in range(2):
                            k = 2 * j + k2
                            w = slice(k2 * 512, k2 * 512 + width)
                            last = three(ps[0:ROWS[t], bank_of(parity, t), 0:width], h_hi[:, k, cols(t)],
                                         h_lo[:, k, cols(t)], w_hi[:, j, w], w_lo[:, j, w], k == 0, k == KD - 1)
                        if j == 3 and t < NT - 1:
                            last.then_inc(tok_done, 1)
                    last.then_inc(unit_done, 1)
                    if between and j in between:
                        between[j]()

            pe.sem_inc(tile_read, 2)
            pe.sem_inc(tok_read, 10)
            pe.sem_inc(mix_read, 4)

            pe.wait_ge(ones_set, 1)
            token_chunk(0, 0, 0, 512, h_count=0,
                        between={2: lambda: norm_sums(0), 3: lambda: norm_spread(0)})
            pe.wait_ge(var_set, 2)
            pe.wait_ge(rms_bc_set, 2)
            for c in range(1, 4):
                token_chunk(c, c % 2, 4 * c, 512)
            with pe.Fori(0, 2, 1) as half:
                pe.reg_mov(filled, half * 48 + 48)
                pe.wait_ge(set_up, SETUPS)
                pe.wait_ge(half_loaded, filled)
                with pe.Fori(0, 2, 1) as i:
                    for u in range(4):
                        f = half * 16 + i * 4 + u
                        g = half * 8 + i * 4 + u
                        m = i * 4 + u
                        feature_tile(u, f, f + U_SGU, H, h_ready, KD)
                        pe.wait_ge(tok_read, 10 + 20)
                        pe.wait_ge(vn_ready, g * 2 + 2)
                        pe.wait_ge(mix_read, g * 2 + 2)
                        b = 4 + 2 * (u % 2)
                        for t in range(NT):
                            r = ROWS[t]
                            out = ps[:, b, t * P:(t + 1) * P] if t < 4 else ps[:, b + 1, 0:DEC]
                            last = nc.tensor.matmul(out, vn[0:r, u % 2, t, :],
                                                    ws_sb[0:r, ds(m, 1), 0:r].rearrange("p o i -> p (o i)"),
                                                    start=True, stop=True)
                        last.then_inc(mix_done, 1)
                with pe.Fori(0, 2, 1) as i:
                    for u in range(4):
                        f = half * 16 + i * 4 + (8 + u)
                        feature_tile(u, f, f + U_SGU, HID, hid_ready, half * 8 + (B_SGU + 8))

            def mlp(f0, n0, b0, h_count, s, spread_n):
                def sums():
                    norm_sums(s)

                for m in range(8):
                    feature_tile(m % 4, f0 + m, n0 + m, H, h_ready, h_count,
                                 middle=(lambda: norm_spread(spread_n)) if m == 1 else None)
                    if m == 0:
                        norm_sums(s)

                def down(q):
                    with pe.Fori(0, 2, 1) as i:
                        for u in range(4):
                            feature_tile(u, q * 16 + i * 4 + (f0 + 8 + u), q * 16 + i * 4 + (n0 + 8 + u),
                                         HID, hid_ready, q * 8 + (b0 + 8))

                down(0)
                with pe.Fori(1, 4, 1) as q:
                    with pe.Fori(0, 2, 1) as i:
                        for u in range(4):
                            feature_tile(u, q * 16 + i * 4 + (f0 + u), q * 16 + i * 4 + (n0 + u),
                                         H, h_ready, h_count)
                    down(q)

            mlp(F_MLP0, U_MLP0, B_MLP0, 2 * KD, 1, 1)

            def turn_latents(pieces):
                for L in pieces:
                    t = L % NT
                    r = ROWS[t]
                    n_k, at = (3, 0) if L < NT else (2, QL)
                    pe.wait_ge(lat_ready, L + 1)
                    if L in (3, 4, 8, 9):
                        pe.wait_ge(lat_split, L - 2)
                    for k in range(n_k):
                        last = nc.tensor.transpose(ps[:, latent_bank(L), k * P:k * P + r],
                                                   lat[0:r, t, at + k * P:at + (k + 1) * P], ident[0:r, 0:r])
                    last.then_inc(lat_turned, 1)

            token_chunk(4, 0, U_IN, QL, between={1: lambda: norm_sums(2)}, h_count=2 * KD, tiles=F_O)
            pe.wait_ge(var_set, 6)
            token_chunk(5, 1, U_IN + 4, KL + ROPE,
                        between={0: lambda: turn_latents(range(0, 3)), 1: lambda: turn_latents(range(3, NT))})

            def gather(pair, g):
                if pair == 0:
                    pe.reg_mov(freed, g * NI + (max(u[1] for u in SCORE_PLAN[("gather", 0)][1]) + 1))
                pe.reg_mov(filled, g * NO + 3 * (pair + 1))
                pe.wait_ge(ident_set, 1)
                pe.wait_ge(o_read, filled)
                if pair == 0:
                    pe.wait_ge(probs_set, freed)
                prompt, sample = gather_psum(pair)
                for t in range(NT):
                    r = ROWS[t]
                    out = prompt[:, 0, t * P:(t + 1) * P] if t < 4 else sample[:, 0, :]
                    last = nc.tensor.transpose(out, o_tok[0:r, pair, t, :], ident[0:r, 0:r])
                    if t >= 3:
                        last.then_inc(o_gathered, 1)

            def head_group(g, first):
                if first:
                    pe.wait_ge(lat_split, NT)
                    pe.wait_ge(tok_read, 10 + 30)
                for k in range(3):
                    pe.wait_ge(split_lo, g * 4 + (U_GRP + k + 1))
                    for t in range(NT):
                        last = three(ps[0:ROWS[t], t, 0:HG * QK], cqT_hi[:, k, cols(t)], cqT_lo[:, k, cols(t)],
                                     w_hi[:, k, 0:HG * QK], w_lo[:, k, 0:HG * QK], k == 0, k == 2)
                        if k == 2 and t < NT - 1:
                            last.then_inc(q_done, 1)
                    last.then_inc(unit_done, 1)
                    if k == 1:
                        if first:
                            turn_latents(range(NT, 2 * NT))
                        else:
                            gather(1, g - 1)
                if first:
                    pe.wait_ge(lat_split, 2 * NT)
                    pe.wait_ge(cache_split, 2)
                pe.wait_ge(split_lo, g * 4 + (U_GRP + 4))

                def turn_keys(j):
                    r = key_rows(j)
                    pe.reg_mov(filled, g * KT_N + (j + 1))
                    pe.reg_mov(freed, g * KT_N + (j - 1) if j >= 2 else g * NT + NT)
                    pe.wait_ge(ident_set, 1)
                    pe.wait_ge(k_ready, filled)
                    pe.wait_ge(kT_set if j >= 2 else q_read, freed)
                    for pair in range(2):
                        last = nc.tensor.transpose(ps[:, 3 + j % 2, pair * P:pair * P + r],
                                                   k_norm[0:r, j % 3, 2 * pair:2 * pair + 2, :].rearrange(
                                                       "p h c -> p (h c)"), ident[0:r, 0:r])
                    last.then_inc(k_turned, 1)

                for j in range(KT_N):
                    r = key_rows(j)
                    keys = slice(key_at(j), key_at(j) + r)
                    if j >= 4:
                        pe.wait_ge(k_ready, g * KT_N + (j - 3))
                    elif j == 3:
                        pe.wait_ge(q_read, g * NT + NT)
                    elif j and not first:
                        pe.wait_ge(hid_ready, g * 2 + B_O)
                    for k in range(2):
                        w = slice(k * 512, (k + 1) * 512)
                        last = three(ps[0:r, key_bank(j), :], cT_hi[:, k, keys], cT_lo[:, k, keys],
                                     w_hi[:, 3, w], w_lo[:, 3, w], k == 0, k == 1)
                    last.then_inc(kv_done if j < KT_N - 1 else unit_done, 1)
                    if j >= 3:
                        turn_keys(j - 3)
                    if first and j == 4:
                        pe.wait_ge(krr_step, 9)
                        for t in range(NT):
                            rk = ROWS[t]
                            out = ps[0:QK, 0, t * P:(t + 1) * P] if t < 4 else ps[0:QK, 1, 0:DEC]
                            last = nc.tensor.transpose(out, krr[0:rk, t, :], ident[0:rk, 0:rk])
                            if t >= 3:
                                last.then_inc(kr_turned, 1)
                    for t in turns_behind(j):
                        if first and t == 0:
                            pe.wait_ge(kr_set, 2)
                        rq = ROWS[t]
                        pe.reg_mov(filled, g * 2 + (1 if t < 4 else 2))
                        if t >= 2:
                            pe.reg_mov(freed, g * NT + (t - 1))
                        pe.wait_ge(ident_set, 1)
                        pe.wait_ge(q_ready, filled)
                        if t >= 2:
                            pe.wait_ge(qT_set, freed)
                        for h in range(HG):
                            last = nc.tensor.transpose(ps[0:QK, t % 2, h * P:h * P + rq], q_tok[0:rq, t, h, :],
                                                       ident[0:rq, 0:rq])
                        last.then_inc(q_turned, 1)

                def score(i):
                    _, a, blk = ITEMS[i]
                    (bank,), (before,) = SCORE_PLAN[("score", i)]
                    if before is None:
                        pe.wait_ge(qT_set, g * NT + NT)
                        if bank == SCORE_BANK + 2:
                            pe.wait_ge(k_ready, g * KT_N + (KT_N - 1))
                    else:
                        pe.wait_ge(probs_set, g * NI + (before[1] + 1))
                    rows = slice(blk * P, (blk + 1) * P)
                    if blk:
                        nc.tensor.matmul(ps[:, bank, 0:blk * P], qT[0:QK, a, rows], kT[0:QK, a, 0:blk * P],
                                         start=True, stop=True)
                    nc.tensor.matmul(ps[:, bank, rows], qT[0:QK + 1, a, rows], kT[0:QK + 1, a, rows],
                                     start=True, stop=True).then_inc(scored, 1)

                def score_samples():
                    pe.wait_ge(kT_set, g * KT_N + KT_N)
                    for pair in range(2):
                        def part(pair, hh, kt, width):
                            at = sample_at(pair, kt)
                            out = sample_scores(pair)[hh * 64:hh * 64 + 64, at:at + width]
                            keys = SEQ + kt * P
                            return nc.tensor.matmul(out, qT[0:QK, 2 * pair + hh, SEQ:T],
                                                    kT[0:QK, 2 * pair + hh, keys:keys + width],
                                                    start=True, stop=True)

                        for hh in range(2):
                            part(pair, hh, 0, 512)
                            last = part(pair, hh, 4, 512)
                        if pair == 0:
                            for owner, hh in ((0, 0), (0, 1), (1, 0), (1, 1)):
                                last = part(owner, hh, 8, DEC)
                        last.then_inc(scored, 1)

                def turn(p):
                    item, tiles = PIECES[p]
                    kind, a, blk = ITEMS[item]
                    needed = item + 1 if p >= RING else max(item + 1, SAMPLE_ITEM + (1 if p < 2 else 2))
                    pe.reg_mov(filled, g * NI + needed)
                    if p >= RING:
                        pe.reg_mov(freed, g * pieces_by(p - RING) + ((p - RING) // 2 + 1))
                    pe.wait_ge(ident_set, 1)
                    pe.wait_ge(probs_set, filled)
                    if p >= RING:
                        pe.wait_ge(piece_set(p - RING), freed)
                    for n, kt in enumerate(tiles):
                        if kind == "prompt":
                            src, w = probs[:, (4 * a + blk) % RING, kt * P:(kt + 1) * P], P
                        else:
                            w = min(P, SKEYS - kt * P)
                            src = probs_s[:, a, sample_at(a, kt):sample_at(a, kt) + w]
                        last = nc.tensor.transpose(ps[0:w, PIECE_BANK + p % RING, n * P:(n + 1) * P], src, ident[:])
                    last.then_inc(piece_turned, 1)

                def times_values(p):
                    item, tiles = PIECES[p]
                    kind, a, blk = ITEMS[item]
                    o = out_of(item)
                    new_output = o >= 2 and tiles[0] == 0 and (kind == "sample" or blk == 0)
                    pe.reg_mov(filled, g * pieces_by(p) + (p // 2 + 1))
                    if new_output:
                        pe.reg_mov(freed, g * NO + (o - 1))
                    elif p == 0:
                        pe.reg_mov(freed, g * KT_N + KT_N)
                    pe.wait_ge(ident_set, 1)
                    pe.wait_ge(piece_set(p), filled)
                    if new_output:
                        pe.wait_ge(o_read, freed)
                    elif p == 0:
                        pe.wait_ge(vals_set, freed)
                    for n, kt in enumerate(tiles):
                        if kind == "prompt":
                            last = nc.tensor.matmul(ps[:, out_bank(o), blk * VD:(blk + 1) * VD],
                                                    turned[:, p % RING, n * P:(n + 1) * P],
                                                    vals[:, kt, a * VD:(a + 1) * VD],
                                                    start=(kt == 0), stop=(kt == blk))
                        else:
                            w = min(P, SKEYS - kt * P)
                            for hh in range(2):
                                h = 2 * a + hh
                                last = nc.tensor.matmul(ps[hh * 64:hh * 64 + 64, out_bank(o), 0:VD],
                                                        turned[0:w, p % RING, n * P + hh * 64:n * P + hh * 64 + 64],
                                                        vals[0:w, 4 + kt, h * VD:(h + 1) * VD],
                                                        start=(kt == 0), stop=(kt == 8))
                    last.then_inc(pv_done, 1)

                if first:
                    pe.wait_ge(rows_loaded, 48)
                pe.wait_ge(kT_set, g * KT_N + 4)
                for step, n in ORDER:
                    if step == "score":
                        score(n)
                    elif step == "samples":
                        score_samples()
                    elif step == "key":
                        turn_keys(n)
                    elif step == "turn":
                        turn(n)
                    elif step == "pv":
                        times_values(n)
                    else:
                        gather(n, g)

            head_group(0, True)
            with pe.Fori(1, NG, 1) as g:
                head_group(g, False)
            gather(1, NG - 1)

            pe.wait_ge(hid_ready, B_O + 8)
            with pe.Fori(0, 2, 1) as i:
                for u in range(4):
                    feature_tile(u, i * 4 + (F_O + u), i * 4 + (U_O + u), HID, hid_ready, B_O + 8)

            mlp(F_MLP1, U_MLP1, B_MLP1, 4 * KD, 3, 2)

        @block.vector
        def _(dve):
            def norm_stats(s):
                dve.wait_ge(stat_summed, s + 1)
                nc.vector.tensor_scalar(var_tok[:, 0:4], ps[:, STAT, 0:4], 1.0 / D, EPS, ALU.mult,
                                        ALU.add).then_inc(var_set, 1)
                nc.vector.tensor_scalar(var_tok[0:DEC, 4:5], ps[0:DEC, STAT, 4:5], 1.0 / D, EPS, ALU.mult,
                                        ALU.add).then_inc(var_set, 1)
                dve.wait_ge(var_set, 2 * s + 2)
                nc.vector.reciprocal(inv_tok[:], var_tok[:]).then_inc(inv_set, 1)

            def norm_diagonal(s):
                dve.wait_ge(rms_set, s + 1)
                for t in range(NT):
                    r = ROWS[t]
                    last = nc.vector.tensor_scalar(diag[0:r, t, 0:r], ident[0:r, 0:r], rms_tok[0:r, t:t + 1], None,
                                                   ALU.mult)
                last.then_inc(diag_set, 1)

            def clear_sums():
                nc.vector.memset(sq_sum[:], 0.0).then_inc(sq_added, 1)

            def next_operand(m, slot, s):
                dve.wait_ge(h_hi_set, m + (8 * s + 1))
                xm, hm, lm = x[:, ds(m, 1), :], h_hi[:, ds(m, 1), :], h_lo[:, ds(m, 1), :]
                nc.vector.scalar_tensor_tensor(out=lm, in0=xm, scalar=gains_sb[:, s, ds(m, 1)],
                                               in1=hm.bitcast(F32), op0=ALU.mult,
                                               op1=ALU.subtract).then_inc(h_ready, 1)
                dve.wait_ge(x_sq, m + (8 * s + 1))
                dve.wait_ge(sq_added, m + (9 * s + 1))
                nc.vector.tensor_tensor(sq_sum[:], sq_sum[:], act_t[:, slot, :], ALU.add).then_inc(sq_added, 1)

            def add_to_x(u, m, f, n):
                dve.wait_ge(unit_done, n + 1)
                dve.wait_ge(tile_read, f + 2)
                xm = x[:, ds(m, 1), :].rearrange("p o (n c) -> p (o n) c", n=2)
                nc.vector.tensor_tensor(xm, tile_psum(u % 2), xm, ALU.add).then_inc(tile_read, 1)

            nc.vector.memset(ws_sb[CHUNK:P, :, 0:CHUNK], 0.0).then_inc(set_up, 1)
            dve.wait_ge(gains_loaded, 16)
            clear_sums()
            for k in range(KD):
                next_operand(k, k % 2, 0)
            dve.wait_ge(set_up, SETUPS)
            dve.wait_ge(ident_set, 1)
            norm_stats(0)
            norm_diagonal(0)

            dve.wait_ge(const_loaded, 16 * CONSTS)
            dve.wait_ge(ss_v_set, 4 * NT)
            nc.vector.reduce_sum(ss_v1[:], ss_v[:], AX_X).then_inc(rms_v_step, 1)
            dve.wait_ge(rms_v_step, 1)
            nc.vector.tensor_scalar(ss_v1[:], ss_v1[:], 1.0 / DS, EPS, ALU.mult, ALU.add).then_inc(rms_v_step, 1)
            dve.wait_ge(rms_v_step, 2)
            nc.vector.reciprocal(ss_v1[:], ss_v1[:]).then_inc(rms_v_step, 1)
            dve.wait_ge(rms_v_set, 1)
            dve.wait_ge(rms_bc_set, 2)

            def norm_v(g, slot):
                for tiles, r in ((slice(0, 4), P), (slice(4, 5), DEC)):
                    n = tiles.stop - tiles.start
                    nc.vector.tensor_tensor(vn[0:r, slot, tiles, :], v[0:r, tiles, ds(g * P, P)],
                                            rms_v[0:r, tiles].unsqueeze(2).broadcast_to([r, n, P]),
                                            ALU.mult).then_inc(vn_ready, 1)

            def gate(half):
                dve.wait_ge(half_loaded, half * 48 + 48)
                with dve.Fori(0, 2, 1) as i:
                    for u in range(4):
                        slot = u % 2
                        m = i * 4 + u
                        g = i * 4 + (half * 8 + u)
                        f = i * 4 + (half * 16 + u)
                        if u == 0:
                            norm_v(g, slot)
                        dve.wait_ge(unit_done, f + (U_SGU + 1))
                        nc.vector.tensor_tensor(halves(act_t[:, slot, :]), tile_psum(slot), halves(rms_bc[:]),
                                                ALU.mult).then_inc(tile_read, 1)
                        if u < 3:
                            norm_v(g + 1, 1 - slot)
                        dve.wait_ge(mix_done, g + 1)
                        if u:
                            dve.wait_ge(hid_ready, g)
                        b = 4 + 2 * slot
                        bias = b_bc[:, ds(m, 1), :]
                        nc.vector.scalar_tensor_tensor(
                            out=mixed[:, 0:SEQ].rearrange("p (c i) -> p c i", c=4),
                            in0=ps[:, b, :].rearrange("p (c i) -> p c i", c=4), scalar=sgu_g[:, ds(g, 1)],
                            in1=bias.broadcast_to([P, 4, P]), op0=ALU.mult, op1=ALU.add).then_inc(mix_read, 1)
                        nc.vector.scalar_tensor_tensor(
                            out=mixed[:, SEQ:T].unsqueeze(1), in0=ps[:, b + 1:b + 2, 0:DEC],
                            scalar=sgu_g[:, ds(g, 1)], in1=bias[:, :, 0:DEC], op0=ALU.mult,
                            op1=ALU.add).then_inc(mix_read, 1)
                        dve.wait_ge(u_set, g + 1)
                        dve.wait_ge(mix_read, g * 2 + 6)
                        nc.vector.tensor_tensor(mixed[:], mixed[:], act_t[:, slot, :], ALU.mult).then_inc(y_set, 1)
                        dve.wait_ge(hid_hi_set, g + 1)
                        nc.vector.tensor_tensor(hid_lo[:, ds(m, 1), :], mixed[:].unsqueeze(1),
                                                hid_hi[:, ds(m, 1), :].bitcast(F32),
                                                ALU.subtract).then_inc(hid_ready, 1)

            def project_back(f0, n0, last_s=None):
                if last_s is not None:
                    clear_sums()
                with dve.Fori(0, 2, 1) as i:
                    for u in range(4):
                        m = i * 4 + u
                        add_to_x(u, m, m + f0, m + n0)
                        if last_s is not None:
                            next_operand(m, u % 2, last_s)

            gate(0)
            nc.vector.scalar_tensor_tensor(out=v_out[:], in0=v[0:DEC, 4, :], scalar=rms_v[0:DEC, 4:5],
                                           in1=v_out[:], op0=ALU.mult, op1=ALU.mult).then_inc(v_out_set, 1)
            project_back(8, U_SGU + 8)
            gate(1)
            project_back(24, U_SGU + 24, last_s=1)

            def mlp(f0, n0, b0, s, spread_n, last_s):
                norm_stats(s)
                norm_diagonal(s)
                dve.wait_ge(rms_bc_set, 2 * spread_n + 2)

                def up(q):
                    with dve.Fori(0, 2, 1) as i:
                        for u in range(4):
                            m = i * 4 + u
                            dve.wait_ge(unit_done, q * 16 + m + (n0 + 1))
                            nc.vector.scalar_tensor_tensor(
                                out=halves(act_t[:, u % 2, :]), in0=tile_psum(u % 2), scalar=0.0,
                                in1=halves(rms_bc[:]), op0=ALU.max, op1=ALU.mult).then_inc(tile_read, 1)
                            dve.wait_ge(hid_hi_set, q * 8 + m + (b0 + 1))
                            nc.vector.tensor_tensor(hid_lo[:, ds(m, 1), :], act_t[:, u % 2, :].unsqueeze(1),
                                                    hid_hi[:, ds(m, 1), :].bitcast(F32),
                                                    ALU.subtract).then_inc(hid_ready, 1)

                with dve.Fori(0, 3, 1) as q:
                    up(q)
                    project_back(q * 16 + (f0 + 8), q * 16 + (n0 + 8))
                up(3)
                project_back(f0 + 56, n0 + 56, last_s=last_s)

            mlp(F_MLP0, U_MLP0, B_MLP0, 1, 1, 2)

            dve.wait_ge(stored, 16)
            half = ROPE // 2
            nc.vector.memset(krr[:, :, 0:NOPE], 0.0).then_inc(krr_step, 1)
            nc.vector.scalar_tensor_tensor(out=gq_col[0:NOPE, :], in0=gq_col[0:NOPE, :], scalar=SCALE,
                                           in1=gk_col[0:NOPE, :], op0=ALU.mult, op1=ALU.mult).then_inc(gq_step, 1)
            nc.vector.memset(gq_col[NOPE:QK, :], SCALE).then_inc(gq_step, 1)
            nc.vector.tensor_tensor(cs_q[:, 0], cs_sb[:, 0], gq_row[:].unsqueeze(1).broadcast_to([P, NT, ROPE]),
                                    ALU.mult).then_inc(gq_step, 1)
            for lo, other in ((0, half), (half, 0)):
                nc.vector.tensor_tensor(cs_q[:, 1, :, lo:lo + half], cs_sb[:, 1, :, lo:lo + half],
                                        gq_row[:, other:other + half].unsqueeze(1).broadcast_to([P, NT, half]),
                                        ALU.mult).then_inc(gq_step, 1)
            for k in range(2):
                dve.wait_ge(cache_hi, k + 1)
                nc.vector.tensor_tensor(cT_lo[:, k, SEQ:SEQ + PAST], cache_raw[:, k, :],
                                        cT_hi[:, k, SEQ:SEQ + PAST].bitcast(F32),
                                        ALU.subtract).then_inc(cache_split, 1)
            norm_stats(2)

            def norm_latents(which, steps, roots, sums_wanted):
                parts = [(0, QL), (QL, KL), (QL + KL, ROPE)]
                dve.wait_ge(ss_lat_set, sums_wanted)
                for w in which:
                    nc.vector.tensor_scalar(ss_lat[:, w, :], ss_lat[:, w, :], 1.0 / parts[w][1], EPS, ALU.mult,
                                            ALU.add).then_inc(lat_step, 1)
                dve.wait_ge(lat_step, steps + len(which))
                lo, hi = which[0], which[-1] + 1
                nc.vector.reciprocal(ss_lat[:, lo:hi, :], ss_lat[:, lo:hi, :]).then_inc(lat_step, 1)
                dve.wait_ge(rms_lat_set, roots)
                for w in which:
                    at, width = parts[w]
                    for t in range(NT):
                        r = ROWS[t]
                        piece = lat[0:r, t, at:at + width]
                        nc.vector.scalar_tensor_tensor(out=piece, in0=piece, scalar=rms_lat[0:r, w, t:t + 1],
                                                       in1=lat_g_bc[0:r, at:at + width], op0=ALU.mult,
                                                       op1=ALU.mult).then_inc(lat_ready, 1)

            def split_latents(pieces):
                for L in pieces:
                    r = ROWS[L % NT]
                    hi, lo, at = latent_target(L)
                    n_k = 3 if L < NT else 2
                    dve.wait_ge(lat_hi, L + 1)
                    nc.vector.tensor_tensor(lo[:, :, at:at + r],
                                            ps[:, latent_bank(L), 0:n_k * P].rearrange(
                                                "p (k c) -> p k c", k=n_k)[:, :, 0:r],
                                            hi[:, :, at:at + r].bitcast(F32), ALU.subtract).then_inc(lat_split, 1)

            def rotate_rope_key():
                dve.wait_ge(lat_ready, 3 * NT)
                for tiles, r in ((slice(0, 4), P), (slice(4, 5), DEC)):
                    k_in = lat[0:r, tiles, QL + KL:QL + KL + ROPE]
                    a, b = rope_a[0:r, tiles, 0, :], rope_b[0:r, tiles, 0, :]
                    nc.vector.tensor_tensor(a, k_in, cs_sb[0:r, 0, tiles, :], ALU.mult).then_inc(krr_step, 1)
                    nc.vector.tensor_tensor(b[:, :, 0:half], k_in[:, :, half:ROPE], cs_sb[0:r, 1, tiles, 0:half],
                                            ALU.mult).then_inc(krr_step, 1)
                    nc.vector.tensor_tensor(b[:, :, half:ROPE], k_in[:, :, 0:half], cs_sb[0:r, 1, tiles, half:ROPE],
                                            ALU.mult).then_inc(krr_step, 1)
                dve.wait_ge(krr_step, 7)
                for tiles, r in ((slice(0, 4), P), (slice(4, 5), DEC)):
                    nc.vector.tensor_tensor(krr[0:r, tiles, NOPE:QK], rope_a[0:r, tiles, 0, :],
                                            rope_b[0:r, tiles, 0, :], ALU.add).then_inc(krr_step, 1)

            norm_latents((0,), 0, 1, NT)
            split_latents(range(0, NT))
            norm_latents((1, 2), 2, 2, 3 * NT)

            def gather(pair, g):
                kt = g * 2 + pair
                prompt, sample = gather_psum(pair)
                dve.wait_ge(hid_hi_set, kt + (B_O + 1))
                nc.vector.tensor_tensor(hid_lo[:, ds(kt, 1), 0:SEQ], prompt,
                                        hid_hi[:, ds(kt, 1), 0:SEQ].bitcast(F32), ALU.subtract)
                nc.vector.tensor_tensor(hid_lo[:, ds(kt, 1), SEQ:T], sample,
                                        hid_hi[:, ds(kt, 1), SEQ:T].bitcast(F32), ALU.subtract).then_inc(hid_ready, 1)

            dve.wait_ge(gq_step, 5)
            def head_group(g, first):
                if first:
                    split_latents(range(NT, 2 * NT))
                    rotate_rope_key()
                else:
                    gather(1, g - 1)
                for t in range(NT):
                    r = ROWS[t]
                    dve.wait_ge(q_sq_set, g * NT + (t + 1))
                    nc.vector.reduce_sum(ss_q[0:r, t].rearrange("p h s -> p (h s)"),
                                         q_sq[0:r, t % 2, :].rearrange("p (s c) -> p s c", c=ROPE),
                                         AX_X).then_inc(q_step_d, 1)
                def query_step(n):
                    if n == 0:
                        dve.wait_ge(q_step_d, g * 9 + 5)
                        nc.vector.tensor_tensor(ss_q2[:], ss_q[:, :, :, 0], ss_q[:, :, :, 1],
                                                ALU.add).then_inc(q_step_d, 1)
                    elif n == 1:
                        dve.wait_ge(q_step_d, g * 9 + 6)
                        nc.vector.tensor_scalar(ss_q[:, :, :, 0:2], ss_q2[:].unsqueeze(3).broadcast_to([P, NT, HG, 2]),
                                                1.0 / NOPE, EPS, ALU.mult, ALU.add).then_inc(q_step_d, 1)
                        nc.vector.tensor_scalar(ss_q[:, :, :, 2], ss_q[:, :, :, 2], 1.0 / ROPE, EPS, ALU.mult,
                                                ALU.add).then_inc(q_step_d, 1)
                    else:
                        dve.wait_ge(q_step_d, g * 9 + 8)
                        nc.vector.reciprocal(ss_q[:], ss_q[:]).then_inc(q_step_d, 1)

                def norm_keys(j):
                    r = key_rows(j)
                    dve.wait_ge(rms_k_set, g * KT_N + (j + 1))
                    if j >= 3:
                        dve.wait_ge(k_turned, g * KT_N + (j - 2))
                    nc.vector.tensor_tensor(
                        k_norm[0:r, j % 3], ps[0:r, key_bank(j), 0:HG * NOPE].rearrange("p (h c) -> p h c", h=HG),
                        rms_k[0:r, j % 2].unsqueeze(2).broadcast_to([r, HG, NOPE]), ALU.mult).then_inc(k_ready, 1)

                def take_queries(t):
                    r = ROWS[t]
                    dve.wait_ge(q_turned, g * NT + (t + 1))
                    nc.vector.tensor_scalar(
                        qT[0:QK, :, cols(t)], ps[0:QK, t % 2, :].rearrange("p (h c) -> p h c", h=HG)[:, :, 0:r],
                        gq_col[0:QK, 0:1], None, ALU.mult).then_inc(qT_set, 1)

                for j in range(KT_N):
                    r = key_rows(j)
                    base = g * (3 * KT_N) + 3 * j
                    if j == KT_N - 1:
                        take_queries(4)
                    dve.wait_ge(k_sq_set, g * KT_N + (j + 1))
                    nc.vector.reduce_sum(ss_k[0:r, j % 2], k_sq[0:r, j % 2].rearrange("p (h c) -> p h c", h=HG),
                                         AX_X).then_inc(k_step, 1)
                    if j >= 1:
                        norm_keys(j - 1)
                    else:
                        query_step(0)
                    dve.wait_ge(k_step, base + 1)
                    nc.vector.tensor_scalar(ss_k[:, j % 2], ss_k[:, j % 2], 1.0 / NOPE, EPS, ALU.mult,
                                            ALU.add).then_inc(k_step, 1)
                    if j == 0:
                        query_step(1)
                    dve.wait_ge(k_step, base + 2)
                    nc.vector.reciprocal(ss_k[:, j % 2], ss_k[:, j % 2]).then_inc(k_step, 1)
                    if j == 0:
                        query_step(2)
                    for t in turns_behind(j):
                        if t < 4:
                            take_queries(t)
                norm_keys(KT_N - 1)

                def row_max(i, scores):
                    dve.wait_ge(scored, g * NI + (i + 1))
                    at = stat_of(i)
                    nc.vector.reduce_max(neg_max[:, at:at + 1], scores, AX_X, negate=True).then_inc(max_set, 1)

                for step, n in ORDER:
                    if step == "score":
                        w = (ITEMS[n][2] + 1) * P
                        row_max(n, ps[:, SCORE_PLAN[(step, n)][0][0], 0:w])
                    elif step == "samples":
                        row_max(SAMPLE_ITEM, sample_scores(0))
                        dve.wait_ge(probs_set, g * NI + (SAMPLE_ITEM + 1))
                        row_max(SAMPLE_ITEM + 1, sample_scores(1))
                    elif step == "turn" and n % 2:
                        take_piece(dve, nc.vector.tensor_copy, n, g, piece_odd)
                    elif step == "pv":
                        item, tiles = PIECES[n]
                        kind, a, blk = ITEMS[item]
                        if not (blk == 3 or tiles[-1] == 8):
                            continue
                        o = out_of(item)
                        end = stat_of(item) + 1
                        i0 = end - 4 if kind == "prompt" else end - 1
                        dve.wait_ge(probs_set, g * NI + (item + 1))
                        nc.vector.reciprocal(inv_sums[:, i0:end], sums[:, i0:end]).then_inc(inv_sums_set, 1)
                        dve.wait_ge(inv_sums_set, g * NO + (o + 1))
                        dve.wait_ge(pv_done, g * NP + (n + 1))
                        if kind == "prompt":
                            at = (a % 2) * VD
                            nc.vector.tensor_tensor(
                                o_tok[:, a // 2, 0:4, at:at + VD],
                                ps[:, out_bank(o), 0:4 * VD].rearrange("p (b c) -> p b c", b=4),
                                inv_sums[:, i0:end].unsqueeze(2).broadcast_to([P, 4, VD]),
                                ALU.mult).then_inc(o_read, 1)
                        else:
                            nc.vector.tensor_scalar(o_tok[0:DEC, a, 4, 0:VD], ps[0:DEC, out_bank(o), 0:VD],
                                                    inv_sums[0:DEC, i0:end], None, ALU.mult)
                            nc.vector.tensor_scalar(o_tok[0:DEC, a, 4, VD:2 * VD], ps[DEC:2 * DEC, out_bank(o), 0:VD],
                                                    inv_sums[DEC:2 * DEC, i0:end], None,
                                                    ALU.mult).then_inc(o_read, 1)
                    elif step == "gather":
                        gather(n, g)

            head_group(0, True)
            with dve.Fori(1, NG, 1) as g:
                head_group(g, False)
            gather(1, NG - 1)

            project_back(F_O, U_O, last_s=3)
            mlp(F_MLP1, U_MLP1, B_MLP1, 3, 2, None)

        @block.scalar
        def _(act):
            act.dma_start(gains_sb[:], gains).then_inc(gains_loaded, 16)
            for k in range(0, KD, 2):
                act.dma_start(x[:, k, :], xt[:, k, :]).then_inc(x_loaded[k], 16)

            def load_half(half):
                at = slice(8 * half, 8 * half + 8)
                act.dma_start(ws_sb[0:CHUNK, :, :], ws[0:CHUNK, at, :]).then_inc(half_loaded, 16)
                act.dma_start(ws_sb[CHUNK:P, :, CHUNK:P], ws[CHUNK:P, at, CHUNK:P]).then_inc(half_loaded, 16)
                act.dma_start(b_bc[:], bs[at, :].partition_broadcast(P)).then_inc(half_loaded, 16)

            def operand_and_square(m, slot, s):
                nc.scalar.activation(h_hi[:, ds(m, 1), :], x[:, ds(m, 1), :], ACT.Copy,
                                     scale=gains_sb[:, s, ds(m, 1)]).then_inc(h_hi_set, 1)
                nc.scalar.activation(act_t[:, slot, :].unsqueeze(1), x[:, ds(m, 1), :], ACT.Square).then_inc(x_sq, 1)

            def norm_root(s):
                act.wait_ge(inv_set, s + 1)
                nc.scalar.activation(rms_tok[:], inv_tok[:], ACT.Sqrt).then_inc(rms_set, 1)

            def norm_take(n):
                act.wait_ge(rms_spread, n + 1)
                nc.scalar.copy(rms_bc[:, 0:SEQ], ps[:, 5, :]).then_inc(rms_bc_set, 1)
                nc.scalar.copy(rms_bc[:, SEQ:T], ps[:, 6, 0:DEC]).then_inc(rms_bc_set, 1)

            act.wait_ge(gains_loaded, 16)
            for k in range(KD):
                act.wait_ge(x_loaded[k], 16)
                if k >= 2:
                    act.wait_ge(sq_added, k)
                operand_and_square(k, k % 2, 0)
            for dst, src in ((sgu_g[:], sgu_gcol),
                             (v_out[:], sgu_grow.partition_broadcast(DEC)),
                             (gq_row[:], q_rope_g.partition_broadcast(P)),
                             (gq_col[0:NOPE, :], q_nope_g), (gk_col[0:NOPE, :], k_nope_g),
                             (cs_sb[:], rope_cs)):
                act.dma_start(dst, src).then_inc(const_loaded, 16)
            load_half(0)
            norm_root(0)
            norm_take(0)

            act.wait_ge(rms_set, 1)
            act.wait_ge(set_up, SETUPS)
            with act.Fori(0, 2, 1) as c2:
                for parity in range(2):
                    c = c2 * 2 + parity
                    for t in range(NT):
                        r = ROWS[t]
                        if t < NT - 1:
                            act.wait_ge(tok_done, c * 4 + (t + 1))
                        else:
                            act.wait_ge(unit_done, c * 4 + 4)
                        vc = v[0:r, t, ds(c * 512, 512)]
                        nc.scalar.activation(vc, ps[0:r, bank_of(parity, t), :], ACT.Gelu,
                                             scale=rms_tok[0:r, t:t + 1]).then_inc(tok_read, 1)
                        act.wait_ge(tok_read, c * 5 + (10 + t + 1))
                        nc.scalar.activation(junk[0:r, :], vc, ACT.Square,
                                             accum_out=ss_v[0:r, t, ds(c, 1)]).then_inc(ss_v_set, 1)
            act.wait_ge(rms_v_step, 3)
            nc.scalar.activation(rms_v[:], ss_v1[:], ACT.Sqrt).then_inc(rms_v_set, 1)

            def gate(half):
                with act.Fori(0, 2, 1) as i:
                    for u in range(4):
                        m = i * 4 + u
                        g = i * 4 + (half * 8 + u)
                        act.wait_ge(tile_read, i * 4 + (half * 16 + u + 3))
                        nc.scalar.activation(act_t[:, u % 2, :], act_t[:, u % 2, :], ACT.Gelu).then_inc(u_set, 1)
                        act.wait_ge(y_set, g + 1)
                        nc.scalar.copy(hid_hi[:, ds(m, 1), :], mixed[:].unsqueeze(1)).then_inc(hid_hi_set, 1)

            def operands(s, f0):
                with act.Fori(0, 2, 1) as i:
                    for u in range(4):
                        m = i * 4 + u
                        act.wait_ge(tile_read, m + (f0 + 3))
                        operand_and_square(m, u % 2, s)

            gate(0)
            act.wait_ge(mix_read, 4 + 16)
            load_half(1)
            act.wait_ge(v_out_set, 1)
            act.dma_start(out_v, v_out[:]).then_inc(stored, 16)
            gate(1)
            operands(1, 24)

            def mlp(f0, b0, n_sq, s, spread_n, last_s):
                norm_root(s)
                norm_take(spread_n)
                with act.Fori(0, 4, 1) as q:
                    with act.Fori(0, 2, 1) as i:
                        for u in range(4):
                            m = i * 4 + u
                            act.wait_ge(tile_read, q * 16 + m + (f0 + 3))
                            nc.scalar.activation(act_t[:, u % 2, :], act_t[:, u % 2, :],
                                                 ACT.Square).then_inc(hid_sq, 1)
                            act.wait_ge(hid_sq, q * 8 + m + (n_sq + 1))
                            nc.scalar.copy(hid_hi[:, ds(m, 1), :], act_t[:, u % 2, :].unsqueeze(1)).then_inc(
                                hid_hi_set, 1)
                if last_s is not None:
                    operands(last_s, f0 + 56)

            mlp(F_MLP0, B_MLP0, 0, 1, 1, 2)

            act.dma_start(cache_raw[:], cache_ct).then_inc(cache_loaded, 16)
            act.dma_start(lat_g_bc[:], lat_g.partition_broadcast(P)).then_inc(cache_loaded, 16)
            act.wait_ge(cache_loaded, 32)
            for k in range(2):
                nc.scalar.copy(cT_hi[:, k, SEQ:SEQ + PAST], cache_raw[:, k, :]).then_inc(cache_hi, 1)
            norm_root(2)
            act.wait_ge(rms_set, 3)
            act.wait_ge(set_up, SETUPS)

            def take_latents(pieces):
                for L in pieces:
                    r = ROWS[L % NT]
                    hi, lo, at = latent_target(L)
                    n_k = 3 if L < NT else 2
                    act.wait_ge(lat_turned, L + 1)
                    nc.scalar.copy(hi[:, :, at:at + r],
                                   ps[:, latent_bank(L), 0:n_k * P].rearrange(
                                       "p (k c) -> p k c", k=n_k)[:, :, 0:r]).then_inc(lat_hi, 1)

            parts = [(0, QL), (QL, KL), (QL + KL, ROPE)]
            for c in range(2):
                at, width = (0, QL) if c == 0 else (QL, KL + ROPE)
                for t in range(NT):
                    r = ROWS[t]
                    if t < NT - 1:
                        act.wait_ge(tok_done, 16 + 4 * c + t + 1)
                    else:
                        act.wait_ge(unit_done, U_IN + 4 * c + 4)
                    nc.scalar.activation(lat[0:r, t, at:at + width], ps[0:r, bank_of(c, t), 0:width], ACT.Copy,
                                         scale=rms_tok[0:r, t:t + 1]).then_inc(tok_read, 1)
                    act.wait_ge(tok_read, 30 + 5 * c + t + 1)
                    for w in ((0,), (1, 2))[c]:
                        a, n = parts[w]
                        nc.scalar.activation(junk[0:r, a - at:a - at + n], lat[0:r, t, a:a + n], ACT.Square,
                                             accum_out=ss_lat[0:r, w, t:t + 1]).then_inc(ss_lat_set, 1)
                if c == 0:
                    act.wait_ge(lat_step, 2)
                    nc.scalar.activation(rms_lat[:, 0, :], ss_lat[:, 0, :], ACT.Sqrt).then_inc(rms_lat_set, 1)
                    take_latents(range(0, NT))
            act.wait_ge(lat_step, 5)
            nc.scalar.activation(rms_lat[:, 1:3, :], ss_lat[:, 1:3, :], ACT.Sqrt).then_inc(rms_lat_set, 1)
            act.wait_ge(unit_done, U_GRP)
            act.dma_start(kT[NOPE:QK, :, SEQ:SEQ + PAST],
                          cache_krt.unsqueeze(1).broadcast_to([ROPE, HG, PAST])).then_inc(rows_loaded, 16)
            act.dma_start(kT[QK:QK + 1, :, 0:SEQ], mask_rows[0:1]).then_inc(rows_loaded, 16)
            act.dma_start(qT[QK:QK + 1, :, 0:SEQ], mask_rows[1:2]).then_inc(rows_loaded, 16)

            def take_rope_key():
                act.wait_ge(kr_turned, 1)
                nc.scalar.copy(kT[NOPE:QK, :, 0:SEQ],
                               ps[NOPE:QK, 0:1, :].broadcast_to([ROPE, HG, SEQ])).then_inc(kr_set, 1)
                act.wait_ge(kr_turned, 2)
                nc.scalar.copy(kT[NOPE:QK, :, SEQ + PAST:KEYS],
                               ps[NOPE:QK, 1:2, 0:DEC].broadcast_to([ROPE, HG, DEC])).then_inc(kr_set, 1)
                act.wait_ge(lat_ready, 3 * NT)
                act.wait_ge(krr_step, 9)
                act.dma_start(out_kv[0:SEQ, :].rearrange("(t p) c -> p t c", p=P),
                              lat[:, 0:4, QL:QL + KL]).then_inc(stored, 16)
                act.dma_start(out_kv[SEQ:T, :], lat[0:DEC, 4, QL:QL + KL]).then_inc(stored, 16)
                act.dma_start(out_kr[0:SEQ, :].rearrange("(t p) c -> p t c", p=P),
                              krr[:, 0:4, NOPE:QK]).then_inc(stored, 16)
                act.dma_start(out_kr[SEQ:T, :], krr[0:DEC, 4, NOPE:QK]).then_inc(stored, 16)

            def gather(pair, g):
                kt = g * 2 + pair
                prompt, sample = gather_psum(pair)
                act.wait_ge(stored, 16 * 5)
                act.wait_ge(o_gathered, g * 4 + (2 * pair + 2))
                nc.scalar.copy(hid_hi[:, ds(kt, 1), 0:SEQ], prompt)
                nc.scalar.copy(hid_hi[:, ds(kt, 1), SEQ:T], sample).then_inc(hid_hi_set, 1)

            def head_group(g, first):
                if first:
                    take_latents(range(NT, 2 * NT))
                else:
                    gather(1, g - 1)
                for t in range(NT):
                    r = ROWS[t]
                    if t < NT - 1:
                        act.wait_ge(q_done, g * (NT - 1) + (t + 1))
                    else:
                        act.wait_ge(unit_done, g * 4 + (U_GRP + 3))
                    if t >= 2:
                        act.wait_ge(q_step_d, g * 9 + (t - 1))
                    nc.scalar.activation(q_sq[0:r, t % 2, :], ps[0:r, t, 0:HG * QK], ACT.Square).then_inc(q_sq_set, 1)
                    nc.scalar.copy(q_tok[0:r, t].rearrange("p h c -> p (h c)"),
                                   ps[0:r, t, 0:HG * QK]).then_inc(q_read, 1)

                def key_root(j):
                    act.wait_ge(k_step, g * (3 * KT_N) + (3 * j + 3))
                    nc.scalar.activation(rms_k[:, j % 2], ss_k[:, j % 2], ACT.Sqrt).then_inc(rms_k_set, 1)

                def take_keys(j):
                    r = key_rows(j)
                    act.wait_ge(k_turned, g * KT_N + (j + 1))
                    for hh in range(2):
                        to = kT[0:NOPE].rearrange("p (a b) n -> p a b n", b=2)[:, :, hh, key_at(j):key_at(j) + r]
                        last = nc.scalar.copy(to, ps[hh * NOPE:(hh + 1) * NOPE, 3 + j % 2, 0:2 * P].rearrange(
                            "p (a c) -> p a c", a=2)[:, :, 0:r])
                    last.then_inc(kT_set, 1)

                for j in range(KT_N):
                    r = key_rows(j)
                    b = key_bank(j)
                    if j < KT_N - 1:
                        act.wait_ge(kv_done, g * (KT_N - 1) + (j + 1))
                    else:
                        act.wait_ge(unit_done, g * 4 + (U_GRP + 4))
                    if j >= 2:
                        act.wait_ge(k_step, g * (3 * KT_N) + (3 * (j - 2) + 1))
                    nc.scalar.activation(k_sq[0:r, j % 2, :], ps[0:r, b, 0:HG * NOPE], ACT.Square).then_inc(k_sq_set, 1)
                    if j >= 1:
                        key_root(j - 1)
                    nc.scalar.copy(vals[0:r, j, :], ps[0:r, b, HG * NOPE:512]).then_inc(vals_set, 1)
                    if j == 1:
                        act.wait_ge(q_step_d, g * 9 + 9)
                        nc.scalar.activation(rms_q[:], ss_q[:], ACT.Sqrt).then_inc(rms_q_set, 1)
                    if j >= 3:
                        take_keys(j - 3)
                    if first and j == 5:
                        take_rope_key()
                key_root(KT_N - 1)

                def exponentials(i, dst, src):
                    act.wait_ge(max_set, g * NI + (i + 1))
                    at = stat_of(i)
                    nc.scalar.activation(dst, src, ACT.Exp, bias=neg_max[:, at:at + 1],
                                         accum_out=sums[:, at:at + 1]).then_inc(probs_set, 1)

                for step, n in ACT_ORDER:
                    if step == "score":
                        _, a, blk = ITEMS[n]
                        i = 4 * a + blk
                        w = (blk + 1) * P
                        if i >= RING:
                            before = max(p for p, (item, _) in enumerate(PIECES) if item == ITEMS.index(PROMPT[i - RING]))
                            act.wait_ge(piece_turned, g * NP + (before + 1))
                        exponentials(n, probs[:, i % RING, 0:w], ps[:, SCORE_PLAN[(step, n)][0][0], 0:w])
                    elif step == "samples":
                        for pair in range(2):
                            exponentials(SAMPLE_ITEM + pair, probs_s[:, pair, :], sample_scores(pair))
                    elif step == "key":
                        take_keys(n)
                    elif step == "turn" and n % 2 == 0:
                        take_piece(act, nc.scalar.copy, n, g, piece_even)
                    elif step == "gather":
                        gather(n, g)

            head_group(0, True)
            with act.Fori(1, NG, 1) as g:
                head_group(g, False)
            gather(1, NG - 1)

            operands(3, F_O)
            mlp(F_MLP1, B_MLP1, 32, 3, 2, None)
            with act.Fori(0, KD, 1) as m:
                act.wait_ge(tile_read, m + (F_MLP1 + 56 + 3))
                act.dma_start(out_x[:, ds(m, 1), :], x[:, ds(m, 1), :]).then_inc(stored, 16)
            act.wait_ge(stored, 16 * (5 + KD))


def _units(*blocks):
    out = []
    for w, k_tiles, pitch in blocks:
        u = np.zeros((P, UNIT), np.float32)
        for k in range(k_tiles):
            u[:, k * pitch:k * pitch + w.shape[1]] = w[k * P:(k + 1) * P]
        out.append(u)
    return out


def _feature_major(w, rows, n_tiles):
    return _units(*[(w[rows:rows + 8 * P, m * P:(m + 1) * P], 8, P) for m in range(n_tiles)])


def _weight_stream(sgu_in, sgu_out, up, down, mla_in, uq, ukv, wo):
    units = []
    v_part = sgu_in[:, DS:]
    for c in range(4):
        units += _units(*[(v_part[2 * j * P:2 * (j + 1) * P, c * 512:(c + 1) * 512], 2, 512) for j in range(4)])
    for half in range(2):
        units += _feature_major(sgu_in[:, half * D:(half + 1) * D], 0, 8)
        units += _feature_major(sgu_out, half * D, 8)

    def mlp(layer):
        out = []
        for q in range(4):
            out += _feature_major(up[layer][:, q * D:(q + 1) * D], 0, 8)
            out += _feature_major(down[layer], q * D, 8)
        return out

    units += mlp(0)
    for lo, hi in ((0, QL), (QL, QL + KL + ROPE)):
        units += _units(*[(mla_in[2 * j * P:2 * (j + 1) * P, lo:hi], 2, 512) for j in range(4)])
    kv = ukv.reshape(KL, HEADS, NOPE + VD)
    for g in range(NG):
        heads = slice(g * HG, (g + 1) * HG)
        q_cols = uq[:, g * HG * QK:(g + 1) * HG * QK]
        units += _units(*[(q_cols[k * P:(k + 1) * P], 1, 512) for k in range(3)])
        both = np.concatenate([kv[:, heads, :NOPE].reshape(KL, -1), kv[:, heads, NOPE:].reshape(KL, -1)], 1)
        units += _units((both, 2, 512))
    units += _feature_major(wo, 0, 8)
    units += mlp(1)
    assert len(units) == UNITS
    return np.stack(units)


def _rope_tables():
    half = ROPE // 2
    inv = (np.float32(10000.0) ** (-np.arange(half, dtype=np.float32) / np.float32(half))).astype(np.float32)
    pos = np.concatenate([np.arange(SEQ), PAST + np.arange(DEC)]).astype(np.float32)
    ang = (pos[:, None] * inv[None, :]).astype(np.float32)
    cos, sin = np.cos(ang), np.sin(ang)
    table = np.zeros((P, 2, NT, ROPE), np.float32)
    for t in range(NT):
        r = ROWS[t]
        at = slice(t * P, t * P + r)
        table[:r, 0, t] = np.concatenate([cos[at], cos[at]], 1)
        table[:r, 1, t] = np.concatenate([-sin[at], sin[at]], 1)
    return table


def _mask_rows():
    odd = (np.arange(SEQ) // CHUNK) % 2 == 1
    rows = np.zeros((2, HG, SEQ), np.float32)
    rows[0, :, odd] = MASKED
    rows[1, :, ~odd] = 1.0
    return rows


def kernel(**inputs):
    import concourse.bacc as _bacc
    from concourse.bass_utils import run_bass_kernel_spmd as _run

    a = {k: np.asarray(w) for k, w in inputs.items()}
    tokens = np.concatenate([a["x_prompt"][0], a["x_sample"][0]], 0)
    arrays = {
        "xt": tokens.T.reshape(KD, P, T).transpose(1, 0, 2),
        "gains": np.stack([a["mix_norm_g"][0], a["mlp_norm_g"][0], a["mix_norm_g"][1], a["mlp_norm_g"][1]])
                   .reshape(4, KD, P).transpose(2, 0, 1),
        "stream": _weight_stream(a["sgu_w_in"][0], a["sgu_w_out"][0], a["mlp_w_up"], a["mlp_w_down"],
                                 a["mla_w_in"][0], a["mla_w_uq"][0], a["mla_w_ukv"][0], a["mla_w_o"][0]),
        "ws": a["sgu_w_s"][0].transpose(2, 0, 1),
        "bs": a["sgu_b_s"][0],
        "sgu_gcol": a["sgu_norm_g"][0].reshape(GROUPS, P).T,
        "sgu_grow": a["sgu_norm_g"][0],
        "cache_ct": a["cache_kv_latent"][0, 0].T.reshape(2, P, PAST).transpose(1, 0, 2),
        "cache_krt": a["cache_k_rope"][0, 0].T,
        "lat_g": np.concatenate([a["mla_q_norm_g"][0], a["mla_kv_norm_g"][0], a["mla_k_rope_g"][0]]),
        "q_nope_g": a["mla_q_nope_g"][0][:, None],
        "q_rope_g": a["mla_q_rope_g"][0],
        "k_nope_g": a["mla_k_nope_g"][0][:, None],
        "rope_cs": _rope_tables(),
        "mask_rows": _mask_rows(),
    }
    outs = {"out_x": (P, KD, T), "out_kv": (T, KL), "out_kr": (T, ROPE), "out_v": (DEC, DS)}
    nc = _bacc.Bacc("TRN2", target_bir_lowering=False, num_devices=1, dynamic_dma_scratch_size=1024)
    args = {}
    for name, value in arrays.items():
        arrays[name] = value = np.ascontiguousarray(value)
        args[name] = nc.dram_tensor(name, value.shape, mybir.dt.from_np(value.dtype), kind="ExternalInput").ap()
    for name, shape in outs.items():
        args[name] = nc.dram_tensor(name, shape, F32, kind="ExternalOutput").ap()
    build_trunk(nc, **args)
    r = _run(nc, [arrays], core_ids=[0]).results[0]
    y = r["out_x"].transpose(1, 0, 2).reshape(D, T).T
    kv, kr = r["out_kv"], r["out_kr"]
    return (y[None, :SEQ], y[None, SEQ:], kv[None, None, :SEQ], kr[None, None, :SEQ], kv[None, None, SEQ:],
            kr[None, None, SEQ:], r["out_v"][None, None])
```
